# Optimizing a Trainium2 kernel written in Bass

```python
import jax, jax.numpy as jnp
from jax import lax
import numpy as np

D_MODEL = 1024
BATCH = 1
SEQ = 256
DEPTH = 2

GRID_W = 64
N_META = 16
N_MIXERS = 2
NA_HEADS = 16
NA_HEAD_DIM = D_MODEL // NA_HEADS
NA_WIN_ROWS = 8
NA_WIN_COLS = 16
GQA_HEADS = 16
GQA_KV_HEADS = 4
GQA_GROUP = GQA_HEADS // GQA_KV_HEADS
GQA_HEAD_DIM = D_MODEL // GQA_HEADS
Q_BLOCK = 128
ROPE_THETA = 10000.0
D_FF = 2816
RMS_EPS = 1e-6
N_NA_LAYERS = (DEPTH + 1) // 2
N_GQA_LAYERS = DEPTH // 2

kernel_name = "hybrid_natten_gqa_macaron_encoder"

def rms_norm(x, gain):
    xf = x.astype(jnp.float32)
    y = xf * lax.rsqrt(jnp.mean(xf * xf, axis=-1, keepdims=True) + RMS_EPS)
    return (y * gain.astype(jnp.float32)).astype(x.dtype)

def swiglu(x, w_gate, w_up, w_down):
    return (jax.nn.silu(x @ w_gate) * (x @ w_up)) @ w_down

def neighborhood_attention(h, w_qkv, w_o, rpb, meta_bias):
    b, l, d = h.shape
    n = l - N_META
    rows = n // GRID_W
    kh = min(NA_WIN_ROWS, rows)
    kw = NA_WIN_COLS
    qkv = (h @ w_qkv).reshape(b, l, 3, NA_HEADS, NA_HEAD_DIM)
    q = qkv[:, :, 0] * (NA_HEAD_DIM ** -0.5)
    k = qkv[:, :, 1]
    v = qkv[:, :, 2]
    q_m, k_m, v_m = q[:, :N_META], k[:, :N_META], v[:, :N_META]
    q_g = q[:, N_META:].reshape(b, rows, GRID_W, NA_HEADS, NA_HEAD_DIM)
    k_g = k[:, N_META:].reshape(b, rows, GRID_W, NA_HEADS, NA_HEAD_DIM)
    v_g = v[:, N_META:].reshape(b, rows, GRID_W, NA_HEADS, NA_HEAD_DIM)

    s_mm = jnp.einsum('bqhd,bkhd->bhqk', q_m, k_m).astype(jnp.float32)
    p_mm = jax.nn.softmax(s_mm, axis=-1).astype(v.dtype)
    o_meta = jnp.einsum('bhqk,bkhd->bqhd', p_mm, v_m).reshape(b, N_META, d)

    cols = np.arange(GRID_W)
    col_start = np.clip(cols - kw // 2, 0, GRID_W - kw)
    col_idx = col_start[:, None] + np.arange(kw)[None, :]
    col_rel = col_idx - cols[:, None] + (NA_WIN_COLS - 1)
    rpb_cols = rpb[:, :, col_rel].astype(jnp.float32)
    mbias = meta_bias.astype(jnp.float32)[None, :, None, :]

    def row_block(r):
        rs = jnp.clip(r - kh // 2, 0, rows - kh)
        q_r = lax.dynamic_index_in_dim(q_g, r, axis=1, keepdims=False)
        k_band = lax.dynamic_slice_in_dim(k_g, rs, kh, axis=1)
        v_band = lax.dynamic_slice_in_dim(v_g, rs, kh, axis=1)
        k_win = k_band[:, :, col_idx]
        v_win = v_band[:, :, col_idx]
        row_rel = rs + jnp.arange(kh) - r + (NA_WIN_ROWS - 1)
        bias = jnp.take(rpb_cols, row_rel, axis=1).transpose(0, 2, 1, 3)
        s_win = jnp.einsum('bchd,brcjhd->bhcrj', q_r, k_win).astype(jnp.float32) + bias[None]
        s_win = s_win.reshape(b, NA_HEADS, GRID_W, kh * kw)
        s_meta = jnp.einsum('bchd,bmhd->bhcm', q_r, k_m).astype(jnp.float32) + mbias
        p = jax.nn.softmax(jnp.concatenate([s_meta, s_win], axis=-1), axis=-1).astype(v.dtype)
        p_meta = p[..., :N_META]
        p_win = p[..., N_META:].reshape(b, NA_HEADS, GRID_W, kh, kw)
        return (jnp.einsum('bhcm,bmhd->bchd', p_meta, v_m)
                + jnp.einsum('bhcrj,brcjhd->bchd', p_win, v_win))

    o_grid = lax.map(row_block, jnp.arange(rows))
    o_grid = jnp.moveaxis(o_grid, 0, 1).reshape(b, n, d)
    o = jnp.concatenate([o_meta, o_grid], axis=1)
    return o @ w_o

def axial_rope_tables(n):
    t = jnp.arange(n)
    row = (t // GRID_W).astype(jnp.float32)
    col = (t % GRID_W).astype(jnp.float32)
    sec = GQA_HEAD_DIM // 2
    freqs = ROPE_THETA ** (-jnp.arange(0, sec, 2, dtype=jnp.float32) / sec)
    ang = jnp.concatenate([row[:, None] * freqs, col[:, None] * freqs], axis=-1)
    ang = jnp.concatenate([jnp.zeros((N_META, sec), jnp.float32), ang], axis=0)
    ang = ang.reshape(N_META + n, 2, sec // 2)
    return jnp.cos(ang), jnp.sin(ang)

def apply_axial_rope(x, cos, sin):
    quarter = GQA_HEAD_DIM // 4
    xs = x.astype(jnp.float32).reshape(*x.shape[:-1], 2, 2, quarter)
    x1, x2 = xs[..., 0, :], xs[..., 1, :]
    c = cos[None, :, None]
    s = sin[None, :, None]
    out = jnp.stack([x1 * c - x2 * s, x2 * c + x1 * s], axis=-2)
    return out.reshape(x.shape).astype(x.dtype)

def grouped_query_attention(h, w_qkv, w_o, q_gain, k_gain):
    b, l, d = h.shape
    n = l - N_META
    nq = GQA_HEADS * GQA_HEAD_DIM
    nkv = GQA_KV_HEADS * GQA_HEAD_DIM
    qkv = h @ w_qkv
    q = qkv[..., :nq].reshape(b, l, GQA_HEADS, GQA_HEAD_DIM)
    k = qkv[..., nq:nq + nkv].reshape(b, l, GQA_KV_HEADS, GQA_HEAD_DIM)
    v = qkv[..., nq + nkv:].reshape(b, l, GQA_KV_HEADS, GQA_HEAD_DIM)
    q = rms_norm(q, q_gain)
    k = rms_norm(k, k_gain)
    cos, sin = axial_rope_tables(n)
    q = apply_axial_rope(q, cos, sin) * (GQA_HEAD_DIM ** -0.5)
    k = apply_axial_rope(k, cos, sin)
    q = q.reshape(b, l, GQA_KV_HEADS, GQA_GROUP, GQA_HEAD_DIM)

    def attend(q_blk):
        s = jnp.einsum('bqkgd,bskd->bkgqs', q_blk, k).astype(jnp.float32)
        p = jax.nn.softmax(s, axis=-1).astype(v.dtype)
        return jnp.einsum('bkgqs,bskd->bqkgd', p, v)

    o_meta = attend(q[:, :N_META]).reshape(b, N_META, nq)
    q_blocks = q[:, N_META:].reshape(b, n // Q_BLOCK, Q_BLOCK, GQA_KV_HEADS, GQA_GROUP, GQA_HEAD_DIM)
    o_blocks = lax.map(attend, jnp.swapaxes(q_blocks, 0, 1))
    o_real = jnp.swapaxes(o_blocks, 0, 1).reshape(b, n, nq)
    o = jnp.concatenate([o_meta, o_real], axis=1)
    return o @ w_o

def setup_inputs(seed: int = 0) -> dict:
    key = jax.random.key(seed)
    ks = jax.random.split(key, 16)
    f32 = jnp.float32
    d, f = D_MODEL, D_FF
    nq = GQA_HEADS * GQA_HEAD_DIM
    nkv = GQA_KV_HEADS * GQA_HEAD_DIM
    return {
        "x": jax.random.normal(ks[0], (BATCH, SEQ, d), f32),
        "meta_tokens": jax.random.normal(ks[1], (N_META, d), f32),
        "norm_gains": 1.0 + 0.05 * jax.random.normal(ks[2], (DEPTH, 6, d), f32),
        "ffn_w_gate": jax.random.normal(ks[3], (DEPTH, 2, d, f), f32) * d ** -0.5,
        "ffn_w_up": jax.random.normal(ks[4], (DEPTH, 2, d, f), f32) * d ** -0.5,
        "ffn_w_down": jax.random.normal(ks[5], (DEPTH, 2, f, d), f32) * f ** -0.5,
        "na_w_qkv": jax.random.normal(ks[6], (N_NA_LAYERS, d, 3 * d), f32) * d ** -0.5,
        "na_w_o": jax.random.normal(ks[7], (N_NA_LAYERS, d, d), f32) * d ** -0.5,
        "na_rpb": 0.1 * jax.random.normal(ks[8], (N_NA_LAYERS, NA_HEADS, 2 * NA_WIN_ROWS - 1, 2 * NA_WIN_COLS - 1), f32),
        "na_meta_bias": 0.1 * jax.random.normal(ks[9], (N_NA_LAYERS, NA_HEADS, N_META), f32),
        "gqa_w_qkv": jax.random.normal(ks[10], (N_GQA_LAYERS, d, nq + 2 * nkv), f32) * d ** -0.5,
        "gqa_w_o": jax.random.normal(ks[11], (N_GQA_LAYERS, nq, d), f32) * nq ** -0.5,
        "gqa_q_gain": 1.0 + 0.05 * jax.random.normal(ks[12], (N_GQA_LAYERS, GQA_HEAD_DIM), f32),
        "gqa_k_gain": 1.0 + 0.05 * jax.random.normal(ks[13], (N_GQA_LAYERS, GQA_HEAD_DIM), f32),
    }

def reference(x, meta_tokens, norm_gains, ffn_w_gate, ffn_w_up, ffn_w_down,
              na_w_qkv, na_w_o, na_rpb, na_meta_bias,
              gqa_w_qkv, gqa_w_o, gqa_q_gain, gqa_k_gain):
    b = x.shape[0]
    meta = jnp.broadcast_to(meta_tokens[None].astype(x.dtype), (b, N_META, D_MODEL))
    h = jnp.concatenate([meta, x], axis=1)
    for i in range(DEPTH):
        g = norm_gains[i]
        ff = swiglu(rms_norm(h, g[0]), ffn_w_gate[i, 0], ffn_w_up[i, 0], ffn_w_down[i, 0])
        h = h + 0.5 * rms_norm(ff, g[1])
        m_in = rms_norm(h, g[2])
        j = i // N_MIXERS
        if i % N_MIXERS == 0:
            m = neighborhood_attention(m_in, na_w_qkv[j], na_w_o[j], na_rpb[j], na_meta_bias[j])
        else:
            m = grouped_query_attention(m_in, gqa_w_qkv[j], gqa_w_o[j], gqa_q_gain[j], gqa_k_gain[j])
        h = h + rms_norm(m, g[3])
        ff = swiglu(rms_norm(h, g[4]), ffn_w_gate[i, 1], ffn_w_up[i, 1], ffn_w_down[i, 1])
        h = h + 0.5 * rms_norm(ff, g[5])
    return h[:, N_META:]


_drawn_inputs = setup_inputs


def setup_inputs(seed=0):
    import zlib

    import numpy as np

    out = dict(_drawn_inputs(seed))
    spreads = {}
    factors = {'gqa_q_gain': 6.238, 'gqa_k_gain': 5.517}
    for name, (base, spread) in spreads.items():
        noise = np.random.default_rng([zlib.crc32(name.encode()), seed]).standard_normal(out[name].shape)
        drawn = base * np.exp(spread * noise) if base else spread * noise
        out[name] = __import__('jax').numpy.asarray(drawn.astype(out[name].dtype))
    for name, factor in factors.items():
        out[name] = (out[name] * factor).astype(out[name].dtype)
    return out
```

```python
from contextlib import ExitStack

import concourse.bass as bass
from concourse import mybir
from concourse.alu_op_type import AluOpType as ALU

F32 = mybir.dt.float32
F32R = mybir.dt.float32r
ACT = mybir.ActivationFunctionType
AX = mybir.AxisListType

P = 128
D = 1024
KC = D // P
FF = 2816
FT = FF // P
GRID_W, GRID_H = 64, 4
GRID = GRID_W * GRID_H
META = 16
TOK = GRID + META
QT = GRID // P
HEADS = 16
HD = 64
DR = 2 * GRID_H - 1
RPB_R, RPB_C = 15, 31
EPS = 1e-6
META_AT = 288
GQA_OUT = (4, 7)
SCALE = HD ** -0.5
BIAS_LOADS = 3 * QT
SLOTS = 4
NARROW, WIDE = KC, FT // 2


SPREAD = P
FIRST_BANKS = (4, 5, 6, 3)
Q_BANKS = (3, 0, 1)
FIRST_ORDER = [("a", 0), ("a", 1), ("b", 0), ("a", 2), ("b", 1), ("a", 3), ("a", 4), ("b", 2), ("a", 5), ("b", 3),
               ("a", 6), ("a", 7), ("b", 4), "mean", ("b", 5), ("b", 6), "spread", ("b", 7)]


def token_tiles(n_tok):
    return [(0, 0), (P, P)] + ([(n_tok - P, 2 * P)] if n_tok > 2 * P else [])


class Segment:

    def __init__(self, name, src, iters, body, blocks, before):
        self.name, self.src, self.iters, self.body, self.blocks = name, src, iters, body, blocks
        self.first = before.first + before.iters * before.body if before else 0
        self.uses = list(before.uses_after) if before else [0] * SLOTS
        self.user = list(before.user_after) if before else [None] * SLOTS
        self.uses_after = [u + (iters if p < body else 0) for p, u in enumerate(self.uses)]
        last = self.first + (iters - 1) * body
        self.user_after = [last + p if p < body else u for p, u in enumerate(self.user)]
        self.next = None
        self.sublayer = None
        if before:
            before.next = self

    def unit(self, i, p):
        return i * self.body + (self.first + p)

    def use(self, i, p):
        return i + (self.uses[p] + 1)

    def former(self, i, p):
        if isinstance(i, int) and i == 0:
            return 0 if self.user[p] is None else self.user[p] + 1
        return (i - 1) * self.body + (self.first + p + 1)


def wait(eng, sem, value):
    if isinstance(value, int) and value <= 0:
        return
    eng.wait_ge(sem, value)


def build(nc, x_t, gains_t, ffn_up_w, ffn_down_w, na_w, na_o_w, gqa_kv_w, gqa_q_w, gqa_o_w,
          rpb, meta_bias, window, ident_c, mean_c, head_mean_c, turn_c, cos_c, sin_c,
          q_gain, k_gain, out):
    segs = []

    def segment(name, src, iters, body, blocks):
        segs.append(Segment(name, src, iters, body, blocks, segs[-1] if segs else None))
        return segs[-1]

    def ffn_segments(f):
        return [segment("up", lambda u, f=f: ffn_up_w[f, u], FT * 2 // 4, 4, NARROW),
                segment("down", lambda u, f=f: ffn_down_w[f, u], KC * 2 // 4, 4, WIDE)]

    plan = {}
    plan["ffn", 0] = ffn_segments(0)
    plan["na"] = segment("na", lambda u: na_w[u], HEADS // 2, 3, NARROW)
    plan["na_o"] = segment("o", lambda u: na_o_w[u], KC // 4, 4, NARROW)
    plan["ffn", 1] = ffn_segments(1)
    plan["ffn", 2] = ffn_segments(2)
    plan["gqa_kv"] = segment("kv", lambda u: gqa_kv_w[u], 1, 4, NARROW)
    plan["gqa_q"] = segment("q", lambda u: gqa_q_w[u], KC // 4, 4, NARROW)
    plan["gqa_o"] = segment("o", lambda u: gqa_o_w[u], KC // 4, 4, NARROW)
    plan["ffn", 3] = ffn_segments(3)
    sublayers = [(0, "ffn", 0, 1, TOK), (1, "na", 2, 3, TOK), (2, "ffn", 4, 5, TOK),
                 (3, "ffn", 6, 7, TOK), (4, "gqa", 8, 9, GRID), (5, "ffn", 10, 11, GRID)]
    ffn_of = {0: 0, 2: 1, 3: 2, 5: 3}
    for n, kind, _, _, _ in sublayers:
        first = plan["na"] if kind == "na" else plan["gqa_kv"] if kind == "gqa" else plan["ffn", ffn_of[n]][0]
        first.sublayer = n

    with ExitStack() as ctx:
        def sb(name, shape, dt=F32):
            return ctx.enter_context(nc.sbuf_tensor(name, shape, dt))

        def sem(name):
            return ctx.enter_context(nc.semaphore(name))

        w_raw = sb("w_raw", [P, SLOTS, WIDE * P])
        w_hi = sb("w_hi", [P, SLOTS, WIDE * P], F32R)
        w_lo = sb("w_lo", [P, SLOTS, WIDE * P], F32R)
        h = sb("h", [P, KC, TOK])
        x_hi = sb("x_hi", [P, KC, TOK], F32R)
        x_lo = sb("x_lo", [P, KC, TOK], F32R)
        y_hi = sb("y_hi", [P, FT, TOK], F32R)
        y_lo = sb("y_lo", [P, FT, TOK], F32R)
        mix = sb("mix", [P, KC, TOK])
        rinv = sb("rinv", [P, TOK])
        sine = sb("sine", [P, TOK])
        sq_sum = sb("sq_sum", [P, TOK])
        in_sq = sb("in_sq", [P, TOK])
        std_rows = sb("std_rows", [P, 3])
        inv_rows = sb("inv_rows", [P, 3])
        out_sq = sb("out_sq", [P, 2, TOK])
        g_sb = sb("g_sb", [P, 2, TOK])
        u_sb = sb("u_sb", [P, 2, TOK])
        s_sb = sb("s_sb", [P, 2, TOK])
        f_sb = sb("f_sb", [P, 2, TOK])
        gains = sb("gains", [P, 12, KC])
        eps = sb("eps", [P, 1])
        ident = sb("ident", [P, P])
        mean_w = sb("mean_w", [P, 1])
        warm = sb("warm", [P, 1])
        head_mean_w = sb("head_mean_w", [P, 2])
        head_std = sb("head_std", [P, 3, 2])
        head_inv = sb("head_inv", [P, 3, 2])
        turn_w = sb("turn_w", [P, P])
        cos_t = sb("cos_t", [P, TOK])
        sin_t = sb("sin_t", [P, TOK])
        win = sb("win", [P, TOK])
        bias_raw = sb("bias_raw", [P, 2, QT, TOK])
        hgain = sb("hgain", [P, 2])
        q_s = sb("q_s", [P, 2, TOK])
        k_s = sb("k_s", [P, 2, TOK])
        vt_s = sb("vt_s", [P, 2, TOK])
        v_s = sb("v_s", [P, 3, 2, P])
        bias = sb("bias", [P, 2, QT, TOK])
        prob = sb("prob", [P, 2, QT, TOK])
        ntop = sb("ntop", [P, 2, QT])
        rows = sb("rows", [P, 2, QT])
        rinv_rows = sb("rinv_rows", [P, 2, QT])
        m_top = sb("m_top", [META, 2])
        m_prob = sb("m_prob", [META, 2, META])
        m_rows = sb("m_rows", [META, 2])
        m_rinv = sb("m_rinv", [META, 2])
        probT = sb("probT", [P, QT, GRID])
        probT_m = sb("probT_m", [META, TOK])
        q_all = sb("q_all", [P, KC, GRID])

        bank = [ctx.enter_context(nc.psum_tensor(f"bank{b}", [P, 512], F32)) for b in range(8)]
        skew = nc.dram_tensor("skew", [HEADS, GRID_W, DR * GRID_W], F32, kind="Internal").ap()

        loaded = [sem(f"loaded{s}") for s in range(SLOTS)]
        w_hi_ready = sem("w_hi_ready")
        w_lo_ready = sem("w_lo_ready")
        unit_done = sem("unit_done")
        x_loaded = [sem(f"x_loaded{s}") for s in range(2)]
        const_loaded = sem("const_loaded")
        const_ready = sem("const_ready")
        skewed = sem("skewed")
        bias_loaded = sem("bias_loaded")
        bias_ready = sem("bias_ready")
        x_hi_ready, x_lo_ready = sem("x_hi_ready"), sem("x_lo_ready")
        h_sq_ready = sem("h_sq_ready")
        pre_mean_done, pre_std_ready, pre_inv_ready = sem("pre_mean_done"), sem("pre_std_ready"), sem("pre_inv_ready")
        pre_spread, rinv_ready, sq_add = sem("pre_spread"), sem("rinv_ready"), sem("sq_add")
        g_ready, u_ready, silu_ready = sem("g_ready"), sem("u_ready"), sem("silu_ready")
        f_ready, y_hi_ready, y_ready = sem("f_ready"), sem("y_hi_ready"), sem("y_ready")
        mix_ready, out_sq_ready, out_sum_ready = sem("mix_ready"), sem("out_sq_ready"), sem("out_sum_ready")
        post_mean_done, post_std_ready, post_inv_ready = sem("post_mean_done"), sem("post_std_ready"), sem("post_inv_ready")
        post_spread, gains_loaded, gains_ready = sem("post_spread"), sem("gains_loaded"), sem("gains_ready")
        delta_ready, h_ready = sem("delta_ready"), sem("h_ready")
        q_ready, k_ready, vt_ready = sem("q_ready"), sem("k_ready"), sem("vt_ready")
        turned, v_ready = sem("turned"), sem("v_ready")
        scores_done, top_ready, biased_ready = sem("scores_done"), sem("top_ready"), sem("biased_ready")
        exp_ready, sum_inv_ready, prob_ready = sem("exp_ready"), sem("sum_inv_ready"), sem("prob_ready")
        probT_done, probT_ready = sem("probT_done"), sem("probT_ready")
        m_scores_done, m_step, m_exp_ready = sem("m_scores_done"), sem("m_step"), sem("m_exp_ready")
        heads_done, o_hi_ready, o_ready = sem("heads_done"), sem("o_hi_ready"), sem("o_ready")
        raw_ready, raw_sq_ready, head_mean_done = sem("raw_ready"), sem("raw_sq_ready"), sem("head_mean_done")
        head_std_ready, head_inv_ready, normed_ready = sem("head_std_ready"), sem("head_inv_ready"), sem("normed_ready")
        head_spread = sem("head_spread")
        turn_done, cos_ready, sin_ready, rope_ready = sem("turn_done"), sem("cos_ready"), sem("sin_ready"), sem("rope_ready")
        q_cur_ready = sem("q_cur_ready")
        stored = sem("stored")

        block = ctx.enter_context(nc.Block())


        def bodies(eng, seg, emit):
            emit(0)
            if seg.iters > 3:
                with eng.Fori(1, seg.iters - 1) as i:
                    emit(i)
            elif seg.iters == 3:
                emit(1)
            if seg.iters > 1:
                emit(seg.iters - 1)

        @block.sync
        def _(sp):
            def load(seg, i, p):
                wait(sp, w_lo_ready, seg.former(i, p))
                sp.dma_start(w_raw[:, p, 0:seg.blocks * P], seg.src(i * seg.body + p)).then_inc(loaded[p], 16)

            def load_bias(c):
                wait(sp, bias_ready, c * 2)
                for t in range(QT):
                    for r in range(2):
                        first_dr = GRID_H - 1 - (2 * t + r)
                        sp.dma_start(bias_raw[GRID_W * r:GRID_W * (r + 1), :, t, 0:GRID],
                                     skew[bass.ds(c * 2, 2), :, first_dr * GRID_W:(first_dr + GRID_H) * GRID_W]
                                     .rearrange("b q k -> q b k")).then_inc(bias_loaded, 16)
                    sp.dma_start(bias_raw[:, :, t, GRID:TOK],
                                 bass.AP(meta_bias.tensor, c * 2 * META, [[0, P], [META, 2], [1, META]])
                                 ).then_inc(bias_loaded, 16)

            for seg in segs:
                if seg.name == "na":
                    sp.wait_ge(skewed, 16 * DR)

                def emit(i):
                    for p in range(seg.body):
                        load(seg, i, p)
                    if seg.name == "na":
                        load_bias(i)
                bodies(sp, seg, emit)
            for c in range(KC):
                sp.wait_ge(h_ready, 5 * KC + c + 1)
                sp.dma_start(out[:, c, :], h[:, c, 0:GRID]).then_inc(stored, 16)
            sp.wait_ge(stored, 16 * KC)

        @block.gpsimd
        def _(pool):
            def split_lo(seg, i, p):
                n = seg.blocks * P
                pool.wait_ge(w_hi_ready, seg.unit(i, p) + 1)
                pool.tensor_tensor(w_lo[:, p, 0:n], w_raw[:, p, 0:n], w_hi[:, p, 0:n].bitcast(F32),
                                   ALU.subtract).then_inc(w_lo_ready, 1)

            def mask(c, b):
                pool.wait_ge(bias_loaded, (c + 1) * (16 * BIAS_LOADS))
                wait(pool, biased_ready, c * 2 + b - 1)
                pool.tensor_tensor(bias[:, b, :, :], bias_raw[:, b, :, :],
                                   win[:, :].unsqueeze(1).to_broadcast([P, QT, TOK]), ALU.add).then_inc(bias_ready, 1)

            def body(seg, i):
                for p in range(2 if isinstance(i, int) and seg.first + i == 0 else 0, seg.body):
                    split_lo(seg, i, p)
                    if seg.name == "na" and p:
                        mask(i, p - 1)

            def sum_squares(n, n_tok):
                for c in range(1, KC):
                    pool.wait_ge(h_sq_ready, n * KC + c + 1)
                    if c > 1:
                        pool.wait_ge(sq_add, n * (KC - 1) + c - 1)
                    pool.tensor_tensor(in_sq[:, 0:n_tok], mix[:, 0, 0:n_tok] if c == 1 else in_sq[:, 0:n_tok],
                                       mix[:, c, 0:n_tok], ALU.add).then_inc(sq_add, 1)

            pool.wait_ge(w_lo_ready, 2)
            for seg in segs:
                body(seg, 0)
                if seg.sublayer is not None:
                    sum_squares(seg.sublayer, TOK if seg.sublayer < 5 else GRID)
                if seg.iters > 1:
                    with pool.Fori(1, seg.iters) as i:
                        body(seg, i)

        @block.scalar
        def _(act):
            act.dma_start(gains[:], gains_t).then_inc(gains_loaded, 16)
            for half in range(2):
                cs = slice(half * KC // 2, (half + 1) * KC // 2)
                act.dma_start(h[:, cs, :], x_t[:, cs, :]).then_inc(x_loaded[half], 16)

            def load_constants():
                for dst, src in ((ident, ident_c), (mean_w, mean_c), (head_mean_w, head_mean_c),
                                 (turn_w, turn_c), (cos_t, cos_c), (sin_t, sin_c), (win, window),
                                 (hgain[:, 0:1], q_gain), (hgain[:, 1:2], k_gain)):
                    act.dma_start(dst if dst.shape == src.shape else dst[:], src).then_inc(const_loaded, 16)

            def skew_biases():
                for d in range(DR):
                    first = (d - (GRID_H - 1) + RPB_R // 2) * RPB_C + RPB_C // 2
                    act.dma_start(skew[:, :, d * GRID_W:(d + 1) * GRID_W], bass.AP(rpb.tensor, first, [[RPB_R * RPB_C, HEADS], [-1, GRID_W], [1, GRID_W]])
                                  ).then_inc(skewed, 16)

            def split_hi(seg, i, p):
                n = seg.blocks * P
                act.wait_ge(loaded[p], seg.use(i, p) * 16)
                wait(act, unit_done, seg.former(i, p))
                act.activation(w_hi[:, p, 0:n], w_raw[:, p, 0:n], ACT.Copy).then_inc(w_hi_ready, 1)

            def ahead(seg, i, p):
                nxt, ni = (seg, i + 1) if not (isinstance(i, int) and i == seg.iters - 1) else (seg.next, 0)
                if nxt is None:
                    return
                for q in [p] if p < seg.body - 1 else range(p, nxt.body):
                    if q < nxt.body:
                        split_hi(nxt, ni, q)

            def prenorm(n, gain, n_tok):
                for c in range(KC):
                    if n == 0:
                        act.wait_ge(x_loaded[c // (KC // 2)], 16)
                    else:
                        act.wait_ge(h_ready, (n - 1) * KC + c + 1)
                    act.activation(x_hi[:, c, 0:n_tok], h[:, c, 0:n_tok], ACT.Copy,
                                   scale=gains[:, gain, c:c + 1]).then_inc(x_hi_ready, 1)
                    act.activation(mix[:, c, 0:n_tok], h[:, c, 0:n_tok], ACT.Square).then_inc(h_sq_ready, 1)
                    if n == 0 and c in (1, 3):
                        split_hi(segs[0], 0, 2 + c // 2)
                if n == 0:
                    skew_biases()

            def pre_std(n, n_tok):
                act.wait_ge(pre_mean_done, n + 1)
                tiles = len(token_tiles(n_tok))
                act.activation(std_rows[:, 0:tiles], bank[7][:, 0:tiles], ACT.Sqrt, bias=eps[:, 0:1]).then_inc(pre_std_ready, 1)

            def pre_rinv(n, n_tok):
                act.wait_ge(pre_spread, n + 1)
                act.activation(rinv[:, 0:n_tok], bank[7][:, SPREAD:SPREAD + n_tok], ACT.Copy).then_inc(rinv_ready, 1)

            def out_square(n, m, par, units, n_tok):
                act.wait_ge(unit_done, units)
                wait(act, out_sum_ready, m + (n * KC - 1))
                act.activation(out_sq[:, par, 0:n_tok], bank[4 + par][:, 0:n_tok], ACT.Square).then_inc(out_sq_ready, 1)

            def post_std(n, n_tok):
                act.wait_ge(post_mean_done, n + 1)
                tiles = len(token_tiles(n_tok))
                act.activation(std_rows[:, 0:tiles], bank[7][:, 0:tiles], ACT.Sqrt, bias=eps[:, 0:1]).then_inc(post_std_ready, 1)

            def out_tiles(n, seg, n_tok):
                units = 2 if seg.name == "down" else 1
                per = seg.body // units

                def emit(i):
                    for t in range(per):
                        ps = range(t * units, (t + 1) * units)
                        last = isinstance(i, int) and i == seg.iters - 1 and t == per - 1
                        if last:
                            for p in ps[:-1]:
                                ahead(seg, i, p)
                            act.activation(warm[:, :], eps[:, :], ACT.Sqrt)
                        out_square(n, i * per + t, t % 2, seg.unit(i, (t + 1) * units - 1) + 1, n_tok)
                        if last:
                            post_std(n, n_tok)
                        for p in ps[-1:] if last else ps:
                            ahead(seg, i, p)
                bodies(act, seg, emit)

            def ffn(n, f, gain, n_tok):
                prenorm(n, gain, n_tok)
                up, down = plan["ffn", f]

                def emit(i):
                    for t in range(2):
                        ahead(up, i, 2 * t)
                        if isinstance(i, int) and i == 0 and t == 0:
                            pre_std(n, n_tok)
                            ahead(up, i, 2 * t + 1)
                            pre_rinv(n, n_tok)
                        tile = i * 2 + (f * FT + t)
                        act.wait_ge(g_ready, tile + 1)
                        act.activation(s_sb[:, t, 0:n_tok], g_sb[:, t, 0:n_tok], ACT.Silu).then_inc(silu_ready, 1)
                        if not (isinstance(i, int) and i == 0 and t == 0):
                            ahead(up, i, 2 * t + 1)
                bodies(act, up, emit)
                out_tiles(n, down, n_tok)

            def probT_copy(e, width, meta_width):
                act.wait_ge(probT_done, e + 1)
                act.activation(probT[:, :, :], bank[5][:, 0:QT * GRID].rearrange("p (a k) -> p a k", a=QT),
                               ACT.Copy).then_inc(probT_ready, 1)
                act.activation(probT_m[:, 0:meta_width], bank[6][0:META, 0:meta_width], ACT.Copy).then_inc(probT_ready, 1)

            def na(n, gain, n_tok):
                prenorm(n, gain, n_tok)
                seg = plan["na"]

                def exps(e, b):
                    act.wait_ge(top_ready, e + 1)
                    for t in range(QT):
                        act.activation(prob[:, b, t, :], prob[:, b, t, :], ACT.Exp, bias=ntop[:, b, t:t + 1],
                                       accum_out=rows[:, b, t:t + 1]).then_inc(exp_ready, 1)

                def former_pair_out(c):
                    act.wait_ge(heads_done, c)
                    act.activation(y_hi[:, bass.ds(c - 1, 1), :], bank[7][:, 0:TOK], ACT.Copy).then_inc(o_hi_ready, 1)

                def emit(c):
                    zero = isinstance(c, int) and c == 0
                    if not zero:
                        probT_copy(c * 2 - 2, GRID, TOK)
                    ahead(seg, c, 0)
                    if zero:
                        pre_std(n, n_tok)
                        ahead(seg, c, 1)
                        pre_rinv(n, n_tok)
                    if not zero:
                        probT_copy(c * 2 - 1, GRID, TOK)
                    exps(c * 2, 0)
                    if not zero:
                        ahead(seg, c, 1)
                    ahead(seg, c, 2)
                    exps(c * 2 + 1, 1)
                    act.wait_ge(m_step, c * 5 + 2)
                    act.activation(m_prob[:, :, :], m_prob[:, :, :], ACT.Exp).then_inc(m_exp_ready, 1)
                    if not zero:
                        former_pair_out(c)
                    act.wait_ge(turned, c + 1)
                    act.activation(v_s[:, 0:2, 0, :], bank[5][:, 0:2 * P].rearrange("p (a k) -> p a k", a=2),
                                   ACT.Copy).then_inc(v_ready, 1)
                    act.activation(v_s[0:META, 2, 0, :], bank[5][0:META, 2 * P:3 * P], ACT.Copy).then_inc(v_ready, 1)
                bodies(act, seg, emit)
                probT_copy(HEADS - 2, GRID, TOK)
                probT_copy(HEADS - 1, GRID, TOK)
                former_pair_out(HEADS // 2)
                out_tiles(n, plan["na_o"], n_tok)

            def gqa(n, gain, n_tok):
                prenorm(n, gain, TOK)
                kv, qs = plan["gqa_kv"], plan["gqa_q"]

                def square(j, w):
                    act.wait_ge(raw_ready, j + 1)
                    wait(act, head_mean_done, j - 1)
                    act.activation(u_sb[:, j % 2, 0:w], g_sb[:, j % 2, 0:w], ACT.Square).then_inc(raw_sq_ready, 1)

                def head_rms(j, w):
                    act.wait_ge(head_mean_done, j + 1)
                    wait(act, head_inv_ready, j)
                    tiles = len(token_tiles(w))
                    act.activation(head_std[:, 0:tiles, :], bank[2][:, 0:2 * tiles].rearrange("p (t b) -> p t b", b=2),
                                   ACT.Sqrt, bias=eps[:, 0:1]).then_inc(head_std_ready, 1)

                ahead(kv, 0, 0)
                pre_std(n, TOK)
                ahead(kv, 0, 1)
                pre_rinv(n, TOK)
                square(0, TOK)
                square(1, TOK)
                ahead(kv, 0, 2)
                for j in range(KC + 2):
                    head_rms(j, TOK if j < 2 else GRID)
                    if j == 0:
                        for x in range(2):
                            act.wait_ge(turned, HEADS // 2 + x + 1)
                            act.activation(v_s[:, 0:2, x, :], bank[5 + x][:, 0:2 * P].rearrange("p (a k) -> p a k", a=2),
                                           ACT.Copy).then_inc(v_ready, 1)
                            act.activation(v_s[0:META, 2, x, :], bank[5 + x][0:META, 2 * P:3 * P], ACT.Copy).then_inc(v_ready, 1)
                        ahead(kv, 0, 3)
                    elif j <= KC:
                        ahead(qs, (j - 1) // 4, (j - 1) % 4)
                    if j < KC:
                        square(j + 2, GRID)

                def step(e, b, do_t, do_s, chunk, x):
                    if do_t:
                        probT_copy(e - 2, GRID, GRID)
                    if do_s:
                        act.wait_ge(top_ready, e + 1)
                        for t in range(QT):
                            act.activation(prob[:, b, t, :], bank[2 * b + t][:, 0:TOK], ACT.Exp, bias=ntop[:, b, t:t + 1],
                                           accum_out=rows[:, b, t:t + 1]).then_inc(exp_ready, 1)
                    if do_t and b == 1:
                        act.wait_ge(heads_done, chunk + HEADS // 2)
                        act.activation(y_hi[:, bass.ds(chunk - 1, 1), 0:GRID], bank[GQA_OUT[1 - x]][:, 0:GRID],
                                       ACT.Copy).then_inc(o_hi_ready, 1)
                for b in range(2):
                    step(HEADS + b, b, False, True, None, 0)
                for b in range(2):
                    step(HEADS + 2 + b, b, True, True, 1, 1)
                with act.Fori(1, HEADS // 4) as j:
                    for x in range(2):
                        for b in range(2):
                            step(j * 4 + (HEADS + 2 * x + b), b, True, True, j * 2 + x, x)
                for b in range(2):
                    step(2 * HEADS + b, b, True, False, KC, 0)
                out_tiles(n, plan["gqa_o"], n_tok)

            split_hi(segs[0], 0, 0)
            split_hi(segs[0], 0, 1)
            load_constants()
            act.wait_ge(gains_ready, 3)
            for n, kind, pre, post, n_tok in sublayers:
                if kind == "ffn":
                    ffn(n, ffn_of[n], pre, n_tok)
                elif kind == "na":
                    na(n, pre, n_tok)
                else:
                    gqa(n, pre, n_tok)

        @block.vector
        def _(dve):
            dve.memset(eps[:, :], EPS).then_inc(gains_ready, 1)
            dve.wait_ge(gains_loaded, 16)
            for post in (1, 5):
                dve.tensor_scalar(gains[:, post:12:6, :], gains[:, post:12:6, :], 0.5, None, ALU.mult).then_inc(gains_ready, 1)
            dve.wait_ge(gains_ready, 3)
            for p in range(2):
                dve.wait_ge(w_hi_ready, p + 1)
                dve.tensor_tensor(w_lo[:, p, 0:D], w_raw[:, p, 0:D], w_hi[:, p, 0:D].bitcast(F32),
                                  ALU.subtract).then_inc(w_lo_ready, 1)

            def x_low(n, gain, c, n_tok):
                dve.wait_ge(x_hi_ready, n * KC + c + 1)
                dve.scalar_tensor_tensor(x_lo[:, c, 0:n_tok], h[:, c, 0:n_tok], gains[:, gain, c:c + 1],
                                         x_hi[:, c, 0:n_tok].bitcast(F32), ALU.mult, ALU.subtract).then_inc(x_lo_ready, 1)

            def input_rinv(n, n_tok):
                tiles = len(token_tiles(n_tok))
                dve.wait_ge(pre_std_ready, n + 1)
                dve.reciprocal(inv_rows[:, 0:tiles], std_rows[:, 0:tiles]).then_inc(pre_inv_ready, 1)
                dve.wait_ge(rinv_ready, n + 1)

            def out_tiles(n, seg, gain, n_tok):
                per = seg.body // (2 if seg.name == "down" else 1)

                def emit(i):
                    for t in range(per):
                        m, par = i * per + t, t % 2
                        dve.wait_ge(unit_done, seg.unit(i, (t + 1) * (seg.body // per) - 1) + 1)
                        dve.wait_ge(out_sq_ready, m + (n * KC + 1))
                        if isinstance(m, int) and m == 0:
                            dve.tensor_copy(sq_sum[:, 0:n_tok], out_sq[:, par, 0:n_tok]).then_inc(out_sum_ready, 1)
                        else:
                            dve.wait_ge(out_sum_ready, m + n * KC)
                            dve.tensor_tensor(sq_sum[:, 0:n_tok], sq_sum[:, 0:n_tok], out_sq[:, par, 0:n_tok],
                                              ALU.add).then_inc(out_sum_ready, 1)
                        dve.tensor_scalar(mix[:, bass.ds(m, 1), 0:n_tok], bank[4 + par][:, 0:n_tok].rearrange("p (a k) -> p a k", a=1),
                                          gains[:, gain, bass.ds(m, 1)], None, ALU.mult).then_inc(mix_ready, 1)
                bodies(dve, seg, emit)

            def update(n, next_gain, n_tok):
                tiles = len(token_tiles(n_tok))
                dve.wait_ge(post_std_ready, n + 1)
                dve.reciprocal(inv_rows[:, 0:tiles], std_rows[:, 0:tiles]).then_inc(post_inv_ready, 1)

                def delta(c):
                    dve.tensor_tensor(mix[:, c, 0:n_tok], mix[:, c, 0:n_tok], bank[7][:, SPREAD:SPREAD + n_tok],
                                      ALU.mult).then_inc(delta_ready, 1)
                dve.wait_ge(post_spread, n + 1)
                dve.wait_ge(mix_ready, (n + 1) * KC)
                delta(0)
                for c in range(KC):
                    if c + 1 < KC:
                        delta(c + 1)
                    dve.wait_ge(delta_ready, n * KC + c + 1)
                    dve.tensor_tensor(h[:, c, 0:n_tok], h[:, c, 0:n_tok], mix[:, c, 0:n_tok], ALU.add).then_inc(h_ready, 1)
                    if c and next_gain is not None:
                        x_low(n + 1, next_gain, c - 1, n_tok)
                if next_gain is not None:
                    x_low(n + 1, next_gain, KC - 1, n_tok)

            def ffn(n, f, post, n_tok):
                input_rinv(n, n_tok)
                up, down = plan["ffn", f]

                def emit(i):
                    banks = FIRST_BANKS if isinstance(i, int) and i == 0 else range(4)
                    for t in range(2):
                        j = i * 2 + t
                        tile = i * 2 + (f * FT + t)
                        dve.wait_ge(unit_done, up.unit(i, 2 * t) + 1)
                        dve.tensor_tensor(g_sb[:, t, 0:n_tok], bank[banks[2 * t]][:, 0:n_tok], rinv[:, 0:n_tok], ALU.mult).then_inc(g_ready, 1)
                        dve.wait_ge(unit_done, up.unit(i, 2 * t + 1) + 1)
                        dve.tensor_tensor(u_sb[:, t, 0:n_tok], bank[banks[2 * t + 1]][:, 0:n_tok], rinv[:, 0:n_tok], ALU.mult).then_inc(u_ready, 1)
                        dve.wait_ge(u_ready, tile + 1)
                        dve.wait_ge(silu_ready, tile + 1)
                        dve.tensor_tensor(f_sb[:, t, 0:n_tok], s_sb[:, t, 0:n_tok], u_sb[:, t, 0:n_tok], ALU.mult).then_inc(f_ready, 1)
                        dve.wait_ge(f_ready, tile + 1)
                        dve.tensor_copy(y_hi[:, bass.ds(j, 1), 0:n_tok], f_sb[:, t:t + 1, 0:n_tok]).then_inc(y_hi_ready, 1)
                        dve.wait_ge(y_hi_ready, tile + 1)
                        dve.tensor_tensor(y_lo[:, bass.ds(j, 1), 0:n_tok], f_sb[:, t:t + 1, 0:n_tok],
                                          y_hi[:, bass.ds(j, 1), 0:n_tok].bitcast(F32), ALU.subtract).then_inc(y_ready, 1)
                bodies(dve, up, emit)
                out_tiles(n, down, post, n_tok)

            def normalise(e, b):
                dve.wait_ge(exp_ready, e * 2 + 2)
                dve.reciprocal(rinv_rows[:, b, :], rows[:, b, :]).then_inc(sum_inv_ready, 1)
                dve.wait_ge(sum_inv_ready, e + 1)
                for t in range(QT):
                    dve.tensor_scalar(prob[:, b, t, :], prob[:, b, t, :], rinv_rows[:, b, t:t + 1], None,
                                      ALU.mult).then_inc(prob_ready, 1)

            def out_low(chunk, ps, o_chunk, n_tok):
                dve.wait_ge(o_hi_ready, chunk)
                dve.tensor_tensor(y_lo[:, bass.ds(o_chunk, 1), 0:n_tok], ps[:, 0:n_tok].rearrange("p (a k) -> p a k", a=1),
                                  y_hi[:, bass.ds(o_chunk, 1), 0:n_tok].bitcast(F32), ALU.subtract).then_inc(o_ready, 1)

            def na(n, post, n_tok):
                input_rinv(n, n_tok)
                seg = plan["na"]

                def value_product(c):
                    dve.wait_ge(unit_done, seg.unit(c, 2) + 1)
                    dve.tensor_tensor(vt_s[:, 0, :], bank[2][:, 0:TOK], rinv[:, :], ALU.mult).then_inc(vt_ready, 1)

                def emit(c):
                    zero = isinstance(c, int) and c == 0
                    dve.wait_ge(unit_done, seg.unit(c, 0) + 1)
                    dve.scalar_tensor_tensor(q_s[:, 0, :], bank[0][:, 0:TOK], SCALE, rinv[:, :], ALU.mult, ALU.mult).then_inc(q_ready, 1)
                    dve.wait_ge(unit_done, seg.unit(c, 1) + 1)
                    dve.tensor_tensor(k_s[:, 0, :], bank[1][:, 0:TOK], rinv[:, :], ALU.mult).then_inc(k_ready, 1)
                    if zero:
                        value_product(c)
                    for b in range(2):
                        e = c * 2 + b
                        if b == 1:
                            if not zero:
                                value_product(c)
                            normalise(c * 2, 0)
                        dve.wait_ge(bias_ready, e + 1)
                        dve.wait_ge(scores_done, e + 1)
                        for t in range(QT):
                            biased = dve.tensor_tensor(prob[:, b, t, :], bank[3 + t][:, 0:TOK], bias[:, b, t, :], ALU.add)
                        biased.then_inc(biased_ready, 1)
                        dve.wait_ge(biased_ready, e + 1)
                        dve.tensor_reduce(ntop[:, b, :], prob[:, b, :, :], AX.X, ALU.max, negate=True).then_inc(top_ready, 1)
                    dve.wait_ge(m_scores_done, c + 1)
                    meta = bank[6][0:META, META_AT:META_AT + 2 * META].rearrange("p (b k) -> p b k", b=2)
                    dve.tensor_reduce(m_top[:, :], meta, AX.X, ALU.max).then_inc(m_step, 1)
                    dve.wait_ge(m_step, c * 5 + 1)
                    wait(dve, probT_done, c * 2)
                    dve.tensor_tensor(m_prob[:, :, :], meta, m_top[:, :].unsqueeze(2).to_broadcast([META, 2, META]),
                                      ALU.subtract).then_inc(m_step, 1)
                    dve.wait_ge(m_exp_ready, c + 1)
                    dve.tensor_reduce(m_rows[:, :], m_prob[:, :, :], AX.X, ALU.add).then_inc(m_step, 1)
                    dve.wait_ge(m_step, c * 5 + 3)
                    dve.reciprocal(m_rinv[:, :], m_rows[:, :]).then_inc(m_step, 1)
                    dve.wait_ge(m_step, c * 5 + 4)
                    dve.tensor_tensor(m_prob[:, :, :], m_prob[:, :, :], m_rinv[:, :].unsqueeze(2).to_broadcast([META, 2, META]),
                                      ALU.mult).then_inc(m_step, 1)
                    if not zero:
                        out_low(c, bank[7], c - 1, TOK)
                    normalise(c * 2 + 1, 1)
                bodies(dve, seg, emit)
                out_low(HEADS // 2, bank[7], HEADS // 2 - 1, TOK)
                out_tiles(n, plan["na_o"], post, n_tok)

            def gqa(n, post, n_tok):
                input_rinv(n, TOK)
                kv, qs = plan["gqa_kv"], plan["gqa_q"]

                def evacuate(j, unit, ps, w):
                    dve.wait_ge(unit_done, unit + 1)
                    dve.tensor_tensor(g_sb[:, j % 2, 0:w], ps[:, 0:w], rinv[:, 0:w], ALU.mult).then_inc(raw_ready, 1)

                def head_rinv(j, w):
                    tiles = len(token_tiles(w))
                    dve.wait_ge(head_std_ready, j + 1)
                    wait(dve, head_spread, j)
                    dve.reciprocal(head_inv[:, 0:tiles, :], head_std[:, 0:tiles, :]).then_inc(head_inv_ready, 1)

                def norm(j, w):
                    dve.wait_ge(head_spread, j + 1)
                    dve.scalar_tensor_tensor(s_sb[:, j % 2, 0:w], g_sb[:, j % 2, 0:w], hgain[:, 1:2] if j < 2 else hgain[:, 0:1],
                                             bank[2][:, SPREAD:SPREAD + w], ALU.mult, ALU.mult).then_inc(normed_ready, 1)
                    dve.wait_ge(normed_ready, j + 1)
                    dve.tensor_tensor(f_sb[:, j % 2, 0:w], s_sb[:, j % 2, 0:w], cos_t[:, 0:w], ALU.mult).then_inc(cos_ready, 1)

                def rope(j, w):
                    dve.wait_ge(turn_done, j + 1)
                    dve.tensor_tensor(sine[:, 0:w], bank[4][:, 0:w], sin_t[:, 0:w], ALU.mult).then_inc(sin_ready, 1)
                    dve.wait_ge(sin_ready, j + 1)
                    dve.wait_ge(cos_ready, j + 1)
                    dst = k_s[:, j, 0:w] if j < 2 else q_all[:, j - 2, 0:w]
                    dve.tensor_tensor(dst, f_sb[:, j % 2, 0:w], sine[:, 0:w], ALU.add).then_inc(rope_ready, 1)

                evacuate(0, kv.unit(0, 0), bank[0], TOK)
                evacuate(1, kv.unit(0, 1), bank[1], TOK)
                for x in range(2):
                    dve.wait_ge(unit_done, kv.unit(0, 2 + x) + 1)
                    dve.tensor_tensor(vt_s[:, x, :], bank[5 + x][:, 0:TOK], rinv[:, :], ALU.mult).then_inc(vt_ready, 1)
                for j in range(KC + 2):
                    w = TOK if j < 2 else GRID
                    head_rinv(j, w)
                    if j:
                        rope(j - 1, TOK if j < 3 else GRID)
                    norm(j, w)
                    if j < KC:
                        evacuate(j + 2, qs.unit(0, 0) + j, bank[Q_BANKS[j % 3]], GRID)
                rope(KC + 1, GRID)
                dve.wait_ge(rope_ready, 10)

                def current(s, x):
                    dve.wait_ge(scores_done, s * 2 + (HEADS - 2))
                    dve.tensor_copy(q_s[:, x:x + 1, 0:GRID], q_all[:, bass.ds(s, 1), :]).then_inc(q_cur_ready, 1)

                def maxima(e, b):
                    dve.wait_ge(scores_done, e + 1)
                    for t in range(QT):
                        red = dve.tensor_reduce(ntop[:, b, t:t + 1], bank[2 * b + t][:, 0:TOK], AX.X, ALU.max, negate=True)
                    red.then_inc(top_ready, 1)

                def chunk(s, x, first):
                    current(s, x)
                    for b in range(2):
                        e = s * 2 + (HEADS + b)
                        if not (first and b == 0):
                            normalise(e - 1, 1 - b)
                        maxima(e, b)
                    if not first:
                        out_low(s + HEADS // 2, bank[GQA_OUT[1 - x]], s - 1, GRID)

                chunk(0, 0, True)
                chunk(1, 1, False)
                with dve.Fori(1, HEADS // 4) as j:
                    for x in range(2):
                        chunk(j * 2 + x, x, False)
                normalise(2 * HEADS - 1, 1)
                out_low(HEADS, bank[GQA_OUT[1]], KC - 1, GRID)
                out_tiles(n, plan["gqa_o"], post, n_tok)

            for c in range(KC):
                dve.wait_ge(x_loaded[c // (KC // 2)], 16)
                x_low(0, 0, c, TOK)
            dve.wait_ge(const_loaded, 16 * 9)
            dve.tensor_scalar(hgain[:, 0:1], hgain[:, 0:1], SCALE, None, ALU.mult).then_inc(const_ready, 1)
            for n, kind, pre, post, n_tok in sublayers:
                if kind == "ffn":
                    ffn(n, ffn_of[n], post, n_tok)
                elif kind == "na":
                    na(n, post, n_tok)
                else:
                    gqa(n, post, n_tok)
                update(n, sublayers[n + 1][2] if n + 1 < len(sublayers) else None, n_tok)

        @block.tensor
        def _(pe):
            def product(ps, seg, p, k, rhs, n_tok, start, stop):
                (hi, lo), r = rhs
                w = slice(k * P, (k + 1) * P)
                pe.matmul(ps[:, 0:n_tok], w_hi[:, p, w], hi[:, r, 0:n_tok], start=start, stop=False)
                pe.matmul(ps[:, 0:n_tok], w_hi[:, p, w], lo[:, r, 0:n_tok], start=False, stop=False)
                return pe.matmul(ps[:, 0:n_tok], w_lo[:, p, w], hi[:, r, 0:n_tok], start=False, stop=stop)

            def unit(seg, i, p, ps, n_tok, act_in, r0=0, start=True, stop=True):
                pe.wait_ge(w_lo_ready, seg.unit(i, p) + 1)
                for k in range(seg.blocks):
                    mm = product(ps, seg, p, k, (act_in, r0 + k), n_tok, start and k == 0, stop and k == seg.blocks - 1)
                mm.then_inc(unit_done, 1)

            X, Y = (x_hi, x_lo), (y_hi, y_lo)

            def token_means(src, n_tok):
                for t, (t0, _) in enumerate(token_tiles(n_tok)):
                    mm = pe.matmul(bank[7][:, t:t + 1], src[:, t0:t0 + P], mean_w[:, :], start=True, stop=True)
                return mm

            def spread(n_tok):
                for t, (t0, first) in enumerate(token_tiles(n_tok)):
                    mm = pe.matmul(bank[7][:, SPREAD + first:SPREAD + t0 + P], inv_rows[:, t:t + 1].to_broadcast([P, P]),
                                   ident[:, first - t0:P], start=True, stop=True)
                return mm

            def first_units(n, seg, banks, n_tok):
                others = range(2, seg.body)
                pe.wait_ge(w_lo_ready, seg.unit(0, 1) + 1)
                waited = False
                for what in FIRST_ORDER:
                    if what == "mean":
                        pe.wait_ge(sq_add, (n + 1) * (KC - 1))
                        pe.wait_ge(const_ready, 1)
                        token_means(in_sq, n_tok).then_inc(pre_mean_done, 1)
                        continue
                    if what == "spread":
                        pe.wait_ge(pre_inv_ready, n + 1)
                        spread(n_tok).then_inc(pre_spread, 1)
                        continue
                    part, k = what
                    if part == "a":
                        pe.wait_ge(x_lo_ready, n * KC + k + 1)
                    elif not waited:
                        pe.wait_ge(w_lo_ready, seg.unit(0, seg.body - 1) + 1)
                        waited = True
                    for p in range(2) if part == "a" else others:
                        mm = product(banks[p], seg, p, k, (X, k), n_tok, k == 0, k == KC - 1)
                        if k == KC - 1:
                            mm.then_inc(unit_done, 1)

            def out_tiles(n, seg, n_tok, ready, before):
                units = 2 if seg.name == "down" else 1
                per = seg.body // units

                def emit(i):
                    zero = isinstance(i, int) and i == 0
                    if zero and units == 1:
                        pe.wait_ge(ready, before + KC - 1)
                        for t in range(2):
                            pe.wait_ge(w_lo_ready, seg.unit(i, t) + 1)
                            for k in range(KC - 1):
                                product(bank[4 + t], seg, t, k, (Y, k), n_tok, k == 0, False)
                        pe.wait_ge(ready, before + KC)
                        for t in range(2):
                            product(bank[4 + t], seg, t, KC - 1, (Y, KC - 1), n_tok, False, True).then_inc(unit_done, 1)
                    for t in range(2 if zero and units == 1 else 0, per):
                        m = i * per + t
                        wait(pe, mix_ready, m + (n * KC - 1))
                        wait(pe, out_sq_ready, m + (n * KC - 1))
                        for k in range(units):
                            if zero and t == 0:
                                pe.wait_ge(ready, before + (k + 1) * seg.blocks)
                            unit(seg, i, t * units + k, bank[4 + t % 2], n_tok, Y, k * seg.blocks, k == 0, k == units - 1)
                bodies(pe, seg, emit)
                pe.wait_ge(out_sum_ready, (n + 1) * KC)
                token_means(sq_sum, n_tok).then_inc(post_mean_done, 1)
                pe.wait_ge(post_inv_ready, n + 1)
                spread(n_tok).then_inc(post_spread, 1)

            def ffn(n, f, n_tok):
                up, down = plan["ffn", f]

                def emit(i):
                    if isinstance(i, int) and i == 0:
                        first_units(n, up, [bank[b] for b in FIRST_BANKS], n_tok)
                        return
                    for t in range(2):
                        tile = i * 2 + (f * FT + t)
                        pe.wait_ge(g_ready, tile - 1)
                        pe.wait_ge(u_ready, tile - 1)
                        unit(up, i, 2 * t, bank[2 * t], n_tok, X)
                        unit(up, i, 2 * t + 1, bank[2 * t + 1], n_tok, X)
                bodies(pe, up, emit)
                out_tiles(n, down, n_tok, y_ready, f * FT)

            def scores(e, b, x, ps):
                at = slice(HD * b, HD * (b + 1))
                for t in range(QT):
                    mm = pe.matmul(ps[t][:, 0:TOK], q_s[at, x[0], t * P:(t + 1) * P], k_s[at, x[1], :], start=True, stop=True)
                mm.then_inc(scores_done, 1)

            def transposed(e, b, meta_queries):
                pe.wait_ge(prob_ready, e * 2 + 2)
                for t in range(QT):
                    for kc in range(2):
                        pe.transpose(bank[5][:, kc * GRID + t * P:kc * GRID + (t + 1) * P],
                                     prob[:, b, t, kc * P:(kc + 1) * P], ident[:, :])
                for t in range(QT):
                    mm = pe.transpose(bank[6][0:META, t * P:(t + 1) * P], prob[:, b, t, GRID:TOK], ident[:, :])
                if meta_queries:
                    mm = pe.transpose(bank[6][0:META, GRID:TOK], m_prob[:, b, :], ident[0:META, 0:META])
                mm.then_inc(probT_done, 1)

            def values(e, b, x, ps, width):
                pe.wait_ge(probT_ready, e * 2 + 2)
                at = slice(HD * b, HD * (b + 1))
                pe.matmul(ps[at, 0:width], v_s[0:META, 2, x, at], probT_m[:, 0:width], start=True, stop=False)
                for kc in range(2):
                    mm = pe.matmul(ps[at, 0:GRID], v_s[:, kc, x, at], probT[:, kc, :], start=False, stop=kc == 1)
                if b == 1:
                    mm.then_inc(heads_done, 1)

            def turn_values(x, vx, ps):
                for kc, (k0, k1) in enumerate(((0, P), (P, 2 * P), (GRID, TOK))):
                    mm = pe.transpose(ps[0:k1 - k0, kc * P:(kc + 1) * P], vt_s[:, x, k0:k1], ident[:, :])
                mm.then_inc(turned, 1)

            def na(n, n_tok):
                seg = plan["na"]

                def head(e, c, b):
                    if b == 0:
                        pe.wait_ge(v_ready, c * 2 + 2)
                        pe.wait_ge(m_step, c * 5 + 5)
                    transposed(e, b, True)

                def meta_scores(b):
                    at = slice(HD * b, HD * (b + 1))
                    return pe.matmul(bank[6][0:META, META_AT + META * b:META_AT + META * (b + 1)], q_s[at, 0, GRID:TOK],
                                     k_s[at, 0, GRID:TOK], start=True, stop=True)

                def blocks_of(c, p, ps, k0, k1):
                    for k in range(k0, k1):
                        mm = product(ps, seg, p, k, (X, k), TOK, k == 0, k == KC - 1)
                    if k1 == KC:
                        mm.then_inc(unit_done, 1)

                def emit(c):
                    zero = isinstance(c, int) and c == 0
                    if zero:
                        first_units(n, seg, bank[0:3], n_tok)
                    else:
                        pe.wait_ge(q_ready, c)
                        unit(seg, c, 0, bank[0], TOK, X)
                        pe.wait_ge(k_ready, c)
                        pe.wait_ge(w_lo_ready, seg.unit(c, 1) + 1)
                        blocks_of(c, 1, bank[1], 0, KC // 2)
                        head(c * 2 - 2, c - 1, 0)
                        blocks_of(c, 1, bank[1], KC // 2, KC)
                        wait(pe, o_ready, c - 1)
                        values(c * 2 - 2, 0, 0, bank[7], TOK)
                    pe.wait_ge(q_ready, c + 1)
                    pe.wait_ge(k_ready, c + 1)
                    wait(pe, biased_ready, c * 2)
                    if zero:
                        meta_scores(0)
                    scores(c * 2, 0, (0, 0), bank[3:5])
                    if not zero:
                        meta_scores(0)
                        head(c * 2 - 1, c - 1, 1)
                        pe.wait_ge(vt_ready, c)
                        unit(seg, c, 2, bank[2], TOK, X)
                        values(c * 2 - 1, 1, 0, bank[7], TOK)
                    pe.wait_ge(biased_ready, c * 2 + 1)
                    scores(c * 2 + 1, 1, (0, 0), bank[3:5])
                    meta_scores(1).then_inc(m_scores_done, 1)
                    pe.wait_ge(vt_ready, c + 1)
                    turn_values(0, 0, bank[5])
                bodies(pe, seg, emit)
                c = HEADS // 2
                head(c * 2 - 2, c - 1, 0)
                pe.wait_ge(o_ready, c - 1)
                values(c * 2 - 2, 0, 0, bank[7], TOK)
                head(c * 2 - 1, c - 1, 1)
                values(c * 2 - 1, 1, 0, bank[7], TOK)
                out_tiles(n, plan["na_o"], n_tok, o_ready, 0)

            def gqa(n, n_tok):
                kv, qs = plan["gqa_kv"], plan["gqa_q"]

                def head_mean(j):
                    w = TOK if j < 2 else GRID
                    pe.wait_ge(raw_sq_ready, j + 1)
                    wait(pe, normed_ready, j)
                    for t, (t0, _) in enumerate(token_tiles(w)):
                        mm = pe.matmul(bank[2][:, 2 * t:2 * t + 2], u_sb[:, j % 2, t0:t0 + P], head_mean_w[:, :], start=True, stop=True)
                    mm.then_inc(head_mean_done, 1)

                def spread_heads(j):
                    pe.wait_ge(head_inv_ready, j + 1)
                    for t, (t0, first) in enumerate(token_tiles(TOK if j < 2 else GRID)):
                        for b in range(2):
                            mm = pe.matmul(bank[2][HD * b:HD * (b + 1), SPREAD + first:SPREAD + t0 + P],
                                           head_inv[:, t, b:b + 1].to_broadcast([P, HD]),
                                           ident[:, first - t0:P], start=True, stop=True)
                    mm.then_inc(head_spread, 1)

                def turn(j):
                    w = TOK if j < 2 else GRID
                    pe.wait_ge(normed_ready, j + 1)
                    wait(pe, sin_ready, j)
                    pe.matmul(bank[4][:, 0:w], turn_w[:, :], s_sb[:, j % 2, 0:w], start=True, stop=True).then_inc(turn_done, 1)

                def q_blocks(s, k0, k1):
                    for k in range(k0, k1):
                        mm = product(bank[Q_BANKS[s % 3]], qs, s % 4, k, (X, k), GRID, k == 0, k == KC - 1)
                    if k1 == KC:
                        mm.then_inc(unit_done, 1)

                first_units(n, kv, [bank[b] for b in (0, 1, 5, 6)], TOK)
                for j in range(KC + 2):
                    if j < KC:
                        wait(pe, raw_ready, j)
                        pe.wait_ge(w_lo_ready, qs.unit(0, 0) + j + 1)
                        q_blocks(j, 0, KC // 2)
                    head_mean(j)
                    if j:
                        turn(j - 1)
                    if j < KC:
                        q_blocks(j, KC // 2, KC)
                    if j == 0:
                        pe.wait_ge(vt_ready, KC + 2)
                        for x in range(2):
                            turn_values(x, x, bank[5 + x])
                    spread_heads(j)
                turn(KC + 1)
                pe.wait_ge(v_ready, HEADS + 4)

                def step(s, x, b, do_s, do_former):
                    e = s * 2 + (HEADS + b)
                    if do_former:
                        transposed(e - 2, b, False)
                    if do_s:
                        if b == 0:
                            pe.wait_ge(q_cur_ready, s + 1)
                        wait(pe, exp_ready, e * 2 - 2)
                        scores(e, b, (x, x), bank[2 * b:2 * b + 2])
                    if do_former:
                        if b == 0:
                            wait(pe, o_ready, s + (HEADS // 2 - 2))
                        values(e - 2, b, 1 - x, bank[GQA_OUT[1 - x]], GRID)

                for s, former in ((0, False), (1, True)):
                    for b in range(2):
                        step(s, s % 2, b, True, former)
                with pe.Fori(1, HEADS // 4) as j:
                    for x in range(2):
                        for b in range(2):
                            step(j * 2 + x, x, b, True, True)
                for b in range(2):
                    step(KC, 0, b, False, True)
                out_tiles(n, plan["gqa_o"], n_tok, o_ready, KC)

            for n, kind, pre, post, n_tok in sublayers:
                if kind == "ffn":
                    ffn(n, ffn_of[n], n_tok)
                elif kind == "na":
                    na(n, n_tok)
                else:
                    gqa(n, n_tok)


def blocks(w, tile_of=None):
    import numpy as np
    k, n = w.shape
    return np.ascontiguousarray(w.reshape(k // P, P, n // P, P).transpose(2, 1, 0, 3)).reshape(n // P, P, k)


def lay_out(a):
    import numpy as np
    f32 = np.float32
    tokens = np.concatenate([a["x"][0], a["meta_tokens"]])
    d = {"x_t": tokens.T.reshape(KC, P, TOK).transpose(1, 0, 2),
         "gains_t": a["norm_gains"].reshape(12, KC, P).transpose(2, 0, 1)}
    gate, up, down = (a[k].reshape(4, *a[k].shape[2:]) for k in ("ffn_w_gate", "ffn_w_up", "ffn_w_down"))
    d["ffn_up_w"] = np.stack([np.stack([blocks(gate[f]), blocks(up[f])], 1).reshape(2 * FT, P, D) for f in range(4)])
    d["ffn_down_w"] = np.stack([blocks(down[f]).reshape(KC, P, 2, WIDE * P).transpose(0, 2, 1, 3)
                                .reshape(2 * KC, P, WIDE * P) for f in range(4)])
    d["na_w"] = blocks(a["na_w_qkv"][0]).reshape(3, KC, P, D).transpose(1, 0, 2, 3).reshape(3 * KC, P, D)
    d["na_o_w"] = blocks(a["na_w_o"][0])
    order = [8 * x + 4 * b + j for j in range(4) for x in range(2) for b in range(2)]
    w = a["gqa_w_qkv"][0]
    wq = w[:, :D].reshape(D, HEADS, HD)[:, order].reshape(D, D)
    d["gqa_kv_w"] = blocks(w[:, D:])
    d["gqa_q_w"] = blocks(wq)
    d["gqa_o_w"] = blocks(a["gqa_w_o"][0].reshape(HEADS, HD, D)[order].reshape(D, D))
    d["rpb"], d["meta_bias"] = a["na_rpb"][0], a["na_meta_bias"][0]
    col = np.arange(GRID_W)
    start = np.clip(col - 8, 0, GRID_W - 16)[:, None]
    inside = (col[None] >= start) & (col[None] < start + 16)
    masked = np.tile(np.where(inside, 0.0, -2.0 ** 100).astype(f32), (2, GRID_H))
    d["window"] = np.concatenate([masked, np.zeros((P, META), f32)], 1)
    d["ident_c"] = np.eye(P, dtype=f32)
    d["mean_c"] = np.full((P, 1), 1.0 / D, f32)
    d["head_mean_c"] = np.kron(np.eye(2), np.full((HD, 1), 1.0 / HD)).astype(f32)
    turn = np.zeros((P, P), f32)
    for m in range(P):
        if m % 32 < 16:
            turn[m + 16, m] = -1.0
        else:
            turn[m - 16, m] = 1.0
    d["turn_c"] = turn
    sec = HD // 2
    freqs = f32(10000.0) ** (-np.arange(0, sec, 2, dtype=f32) / f32(sec))
    t = np.arange(GRID)
    ang = np.stack([(t // GRID_W).astype(f32)[:, None] * freqs, (t % GRID_W).astype(f32)[:, None] * freqs], 1)
    ang = np.concatenate([ang, np.zeros((META, 2, sec // 2), f32)])
    ang = np.tile(np.repeat(ang[:, :, None], 2, 2).reshape(TOK, HD), (1, 2)).T
    d["cos_c"], d["sin_c"] = np.cos(ang, dtype=f32), np.sin(ang, dtype=f32)
    d["q_gain"], d["k_gain"] = (np.tile(a[k][0], 2)[:, None] for k in ("gqa_q_gain", "gqa_k_gain"))
    return {k: np.ascontiguousarray(v) for k, v in d.items()}


_ORDER = ["x_t", "gains_t", "ffn_up_w", "ffn_down_w", "na_w", "na_o_w", "gqa_kv_w", "gqa_q_w", "gqa_o_w",
          "rpb", "meta_bias", "window", "ident_c", "mean_c", "head_mean_c", "turn_c", "cos_c", "sin_c",
          "q_gain", "k_gain"]


def kernel(**inputs):
    import numpy as np
    import concourse.bacc as bacc
    from concourse.bass_utils import run_bass_kernel_spmd

    given = lay_out({k: np.asarray(v) for k, v in inputs.items()})
    nc = bacc.Bacc("TRN2", target_bir_lowering=False, num_devices=1)
    args = [nc.dram_tensor(k, given[k].shape, F32, kind="ExternalInput").ap() for k in _ORDER]
    args.append(nc.dram_tensor("out", (P, KC, GRID), F32, kind="ExternalOutput").ap())
    build(nc, *args)
    got = run_bass_kernel_spmd(nc, [given], core_ids=[0]).results[0]["out"]
    return got.transpose(2, 1, 0).reshape(1, GRID, D)
```

```python
from contextlib import ExitStack

import concourse.bass as bass
from concourse import mybir
from concourse.alu_op_type import AluOpType as ALU

F32 = mybir.dt.float32
F32R = mybir.dt.float32r
ACT = mybir.ActivationFunctionType
AX = mybir.AxisListType

P = 128
D = 1024
KC = D // P
FF = 2816
FT = FF // P
GRID_W, GRID_H = 64, 4
GRID = GRID_W * GRID_H
META = 16
TOK = GRID + META
QT = GRID // P
HEADS = 16
HD = 64
DR = 2 * GRID_H - 1
RPB_R, RPB_C = 15, 31
EPS = 1e-6
META_AT = 288
GQA_OUT = (4, 7)
SCALE = HD ** -0.5
BIAS_LOADS = 3 * QT
X_FIRST = 2
CONST_WIDTHS = (P, 1, 2, P, TOK, TOK, TOK, 2)
VECTOR_SPLITS = ("up", "down")
SLOTS = 4
NARROW, WIDE = KC, FT // 2
SPREAD = P
FIRST_BANKS = (4, 5, 6, 3)
O_BANKS = (0, 1, 4, 5)
Q_BANKS = (3, 0, 1)
START_ORDER = [("a", 0), ("a", 1), ("a", 2), ("a", 3), ("a", 4), ("a", 5), ("b", 0), ("a", 6), ("b", 1), ("a", 7),
               ("b", 2), "mean", ("b", 3), ("b", 4), "spread", ("b", 5), ("b", 6), ("b", 7)]
FIRST_ORDER = [("a", 0), ("b", 0), ("a", 1), ("a", 2), ("b", 1), ("a", 3), ("a", 4), ("b", 2), ("a", 5), ("a", 6), ("b", 3),
               ("a", 7), "mean", ("b", 4), "spread", ("b", 5), ("b", 6), ("b", 7)]


def token_tiles(n_tok):
    return [(0, 0), (P, P)] + ([(n_tok - P, 2 * P)] if n_tok > 2 * P else [])


class Segment:

    def __init__(self, name, src, iters, body, blocks, before):
        self.name, self.src, self.iters, self.body, self.blocks = name, src, iters, body, blocks
        self.first = before.first + before.iters * before.body if before else 0
        self.uses = list(before.uses_after) if before else [0] * SLOTS
        self.user = list(before.user_after) if before else [None] * SLOTS
        self.uses_after = [u + (iters if p < body else 0) for p, u in enumerate(self.uses)]
        last = self.first + (iters - 1) * body
        self.user_after = [last + p if p < body else u for p, u in enumerate(self.user)]
        self.next = None
        self.sublayer = None
        if before:
            before.next = self

    def unit(self, i, p):
        return i * self.body + (self.first + p)

    def use(self, i, p):
        return i + (self.uses[p] + 1)

    def former(self, i, p):
        if isinstance(i, int) and i == 0:
            return 0 if self.user[p] is None else self.user[p] + 1
        return (i - 1) * self.body + (self.first + p + 1)


def out_bank(seg, i, t):
    return O_BANKS[t] if seg.name == "o" and isinstance(i, int) and i == 0 else 4 + t % 2


def wait(eng, sem, value):
    if isinstance(value, int) and value <= 0:
        return
    eng.wait_ge(sem, value)


def build(nc, x_t, gains_t, ffn_up_w, ffn_down_w, na_w, na_o_w, gqa_kv_w, gqa_q_w, gqa_o_w,
          rpb, meta_bias, const_c, out):
    segs = []

    def segment(name, src, iters, body, blocks):
        segs.append(Segment(name, src, iters, body, blocks, segs[-1] if segs else None))
        return segs[-1]

    def ffn_segments(f):
        return [segment("up", lambda u, f=f: ffn_up_w[f, u], FT * 2 // 4, 4, NARROW),
                segment("down", lambda u, f=f: ffn_down_w[f, u], KC * 2 // 4, 4, WIDE)]

    plan = {}
    plan["ffn", 0] = ffn_segments(0)
    plan["na"] = segment("na", lambda u: na_w[u], HEADS // 2, 3, NARROW)
    plan["na_o"] = segment("o", lambda u: na_o_w[u], KC // 4, 4, NARROW)
    plan["ffn", 1] = ffn_segments(1)
    plan["ffn", 2] = ffn_segments(2)
    plan["gqa_kv"] = segment("kv", lambda u: gqa_kv_w[u], 1, 4, NARROW)
    plan["gqa_q"] = segment("q", lambda u: gqa_q_w[u], KC // 4, 4, NARROW)
    plan["gqa_o"] = segment("o", lambda u: gqa_o_w[u], KC // 4, 4, NARROW)
    plan["ffn", 3] = ffn_segments(3)
    sublayers = [(0, "ffn", 0, 1, TOK), (1, "na", 2, 3, TOK), (2, "ffn", 4, 5, TOK),
                 (3, "ffn", 6, 7, TOK), (4, "gqa", 8, 9, GRID), (5, "ffn", 10, 11, GRID)]
    ffn_of = {0: 0, 2: 1, 3: 2, 5: 3}
    for n, kind, _, _, _ in sublayers:
        first = plan["na"] if kind == "na" else plan["gqa_kv"] if kind == "gqa" else plan["ffn", ffn_of[n]][0]
        first.sublayer = n

    with ExitStack() as ctx:
        def sb(name, shape, dt=F32):
            return ctx.enter_context(nc.sbuf_tensor(name, shape, dt))

        def sem(name):
            return ctx.enter_context(nc.semaphore(name))

        w_raw = sb("w_raw", [P, SLOTS, WIDE * P])
        w_hi = sb("w_hi", [P, SLOTS, WIDE * P], F32R)
        w_lo = sb("w_lo", [P, SLOTS, WIDE * P], F32R)
        h = sb("h", [P, KC, TOK])
        x_hi = sb("x_hi", [P, KC, TOK], F32R)
        x_lo = sb("x_lo", [P, KC, TOK], F32R)
        y_hi = sb("y_hi", [P, FT, TOK], F32R)
        y_lo = sb("y_lo", [P, FT, TOK], F32R)
        mix = sb("mix", [P, KC, TOK])
        rinv = sb("rinv", [P, TOK])
        sine = sb("sine", [P, TOK])
        sq_sum = sb("sq_sum", [P, TOK])
        in_sq = sb("in_sq", [P, TOK])
        std_rows = sb("std_rows", [P, 3])
        inv_rows = sb("inv_rows", [P, 3])
        out_sq = sb("out_sq", [P, 2, TOK])
        g_sb = sb("g_sb", [P, 2, TOK])
        u_sb = sb("u_sb", [P, 2, TOK])
        s_sb = sb("s_sb", [P, 2, TOK])
        f_sb = sb("f_sb", [P, 2, TOK])
        gains = sb("gains", [P, 12, KC])
        eps = sb("eps", [P, 1])
        warm = sb("warm", [P, 1])
        idle = sb("idle", [P, P])
        const = sb("const", [P, sum(CONST_WIDTHS)])
        at = [sum(CONST_WIDTHS[:i]) for i in range(len(CONST_WIDTHS) + 1)]
        ident, mean_w, head_mean_w, turn_w, cos_t, sin_t, win, hgain = (
            const[:, a:b] for a, b in zip(at, at[1:]))
        head_std = sb("head_std", [P, 3, 2])
        head_inv = sb("head_inv", [P, 3, 2])
        bias_raw = sb("bias_raw", [P, 2, QT, TOK])
        q_s = sb("q_s", [P, 2, TOK])
        k_s = sb("k_s", [P, 2, TOK])
        vt_s = sb("vt_s", [P, 2, TOK])
        v_s = sb("v_s", [P, 3, 2, P])
        bias = sb("bias", [P, 2, QT, TOK])
        prob = sb("prob", [P, 2, QT, TOK])
        ntop = sb("ntop", [P, 2, QT])
        rows = sb("rows", [P, 2, QT])
        rinv_rows = sb("rinv_rows", [P, 2, QT])
        m_top = sb("m_top", [META, 2])
        m_prob = sb("m_prob", [META, 2, META])
        m_rows = sb("m_rows", [META, 2])
        m_rinv = sb("m_rinv", [META, 2])
        probT = sb("probT", [P, 2, QT, GRID])
        probT_m = sb("probT_m", [META, 2, TOK])
        q_all = sb("q_all", [P, KC, GRID])

        bank = [ctx.enter_context(nc.psum_tensor(f"bank{b}", [P, 512], F32)) for b in range(8)]
        skew = nc.dram_tensor("skew", [HEADS, GRID_W, DR * GRID_W], F32, kind="Internal").ap()

        loaded = [sem(f"loaded{s}") for s in range(SLOTS)]
        w_hi_ready = sem("w_hi_ready")
        w_lo_ready = sem("w_lo_ready")
        unit_done = sem("unit_done")
        x_loaded = [sem(f"x_loaded{s}") for s in range(2)]
        const_loaded = sem("const_loaded")
        const_ready = sem("const_ready")
        skewed = sem("skewed")
        bias_loaded = sem("bias_loaded")
        bias_ready = sem("bias_ready")
        x_hi_ready, x_lo_ready = sem("x_hi_ready"), sem("x_lo_ready")
        h_sq_ready = sem("h_sq_ready")
        pre_mean_done, pre_std_ready, pre_inv_ready = sem("pre_mean_done"), sem("pre_std_ready"), sem("pre_inv_ready")
        pre_spread, rinv_ready, sq_add = sem("pre_spread"), sem("rinv_ready"), sem("sq_add")
        g_ready, u_ready, silu_ready = sem("g_ready"), sem("u_ready"), sem("silu_ready")
        f_ready, y_hi_ready, y_ready = sem("f_ready"), sem("y_hi_ready"), sem("y_ready")
        mix_ready, out_sq_ready, out_sum_ready = sem("mix_ready"), sem("out_sq_ready"), sem("out_sum_ready")
        post_mean_done, post_std_ready, post_inv_ready = sem("post_mean_done"), sem("post_std_ready"), sem("post_inv_ready")
        post_spread, gains_loaded, gains_ready = sem("post_spread"), sem("gains_loaded"), sem("gains_ready")
        delta_ready, h_ready = sem("delta_ready"), sem("h_ready")
        q_ready, k_ready, vt_ready = sem("q_ready"), sem("k_ready"), sem("vt_ready")
        turned, v_ready = sem("turned"), sem("v_ready")
        scores_done, top_ready, biased_ready = sem("scores_done"), sem("top_ready"), sem("biased_ready")
        exp_ready, sum_inv_ready, prob_ready = sem("exp_ready"), sem("sum_inv_ready"), sem("prob_ready")
        probT_done, probT_ready = sem("probT_done"), sem("probT_ready")
        m_scores_done, m_step, m_exp_ready = sem("m_scores_done"), sem("m_step"), sem("m_exp_ready")
        heads_done, o_hi_ready, o_ready = sem("heads_done"), sem("o_hi_ready"), sem("o_ready")
        raw_ready, raw_sq_ready, head_mean_done = sem("raw_ready"), sem("raw_sq_ready"), sem("head_mean_done")
        head_std_ready, head_inv_ready, normed_ready = sem("head_std_ready"), sem("head_inv_ready"), sem("normed_ready")
        head_spread = sem("head_spread")
        turn_done, cos_ready, sin_ready, rope_ready = sem("turn_done"), sem("cos_ready"), sem("sin_ready"), sem("rope_ready")
        q_cur_ready = sem("q_cur_ready")
        idle_ready, stored = sem("idle_ready"), sem("stored")

        block = ctx.enter_context(nc.Block())

        def bodies(eng, seg, emit):
            emit(0)
            if seg.iters > 3:
                with eng.Fori(1, seg.iters - 1) as i:
                    emit(i)
            elif seg.iters == 3:
                emit(1)
            if seg.iters > 1:
                emit(seg.iters - 1)

        @block.sync
        def _(sp):
            def load(seg, i, p):
                wait(sp, w_lo_ready, seg.former(i, p))
                sp.dma_start(w_raw[:, p, 0:seg.blocks * P], seg.src(i * seg.body + p)).then_inc(loaded[p], 16)

            def load_bias(c):
                wait(sp, bias_ready, c * 2)
                for t in range(QT):
                    for r in range(2):
                        first_dr = GRID_H - 1 - (2 * t + r)
                        sp.dma_start(bias_raw[GRID_W * r:GRID_W * (r + 1), :, t, 0:GRID],
                                     skew[bass.ds(c * 2, 2), :, first_dr * GRID_W:(first_dr + GRID_H) * GRID_W]
                                     .rearrange("b q k -> q b k")).then_inc(bias_loaded, 16)
                    sp.dma_start(bias_raw[:, :, t, GRID:TOK],
                                 bass.AP(meta_bias.tensor, c * 2 * META, [[0, P], [META, 2], [1, META]])
                                 ).then_inc(bias_loaded, 16)

            def skew_biases(d):
                first = (d - (GRID_H - 1) + RPB_R // 2) * RPB_C + RPB_C // 2
                sp.dma_start(skew[:, :, d * GRID_W:(d + 1) * GRID_W],
                             bass.AP(rpb.tensor, first, [[RPB_R * RPB_C, HEADS], [-1, GRID_W], [1, GRID_W]])
                             ).then_inc(skewed, 16)

            for seg in segs:
                if seg.name == "na":
                    sp.wait_ge(skewed, 16 * DR)

                def emit(i):
                    for p in range(seg.body):
                        load(seg, i, p)
                        if seg is segs[0] and isinstance(i, int) and i == seg.iters - 1:
                            skew_biases(p)
                        if seg is segs[1] and isinstance(i, int) and i == 0 and 4 + p < DR:
                            skew_biases(4 + p)
                    if seg.name == "na":
                        load_bias(i)
                    if seg is segs[0] and isinstance(i, int) and i == 0:
                        sp.dma_start(const[:], const_c).then_inc(const_loaded, 16)
                bodies(sp, seg, emit)
            for c in range(KC):
                sp.wait_ge(h_ready, 5 * KC + c + 1)
                sp.dma_start(out[:, c, :], h[:, c, 0:GRID]).then_inc(stored, 16)
            sp.wait_ge(stored, 16 * KC)

        @block.gpsimd
        def _(pool):
            def split_lo(seg, i, p):
                n = seg.blocks * P
                pool.wait_ge(w_hi_ready, seg.unit(i, p) + 1)
                pool.tensor_tensor(w_lo[:, p, 0:n], w_raw[:, p, 0:n], w_hi[:, p, 0:n].bitcast(F32),
                                   ALU.subtract).then_inc(w_lo_ready, 1)

            def mask(c, b):
                pool.wait_ge(bias_loaded, (c + 1) * (16 * BIAS_LOADS))
                wait(pool, biased_ready, c * 2 + b - 1)
                pool.tensor_tensor(bias[:, b, :, :], bias_raw[:, b, :, :],
                                   win[:, :].unsqueeze(1).to_broadcast([P, QT, TOK]), ALU.add).then_inc(bias_ready, 1)

            def body(seg, i):
                zero = isinstance(i, int) and i == 0
                first = 2 if zero and seg is segs[0] else 1 if not zero and seg.name in VECTOR_SPLITS else 0
                if first:
                    pool.wait_ge(w_lo_ready, seg.unit(i, first))
                for p in range(first, seg.body):
                    split_lo(seg, i, p)
                    if seg.name == "na" and p:
                        mask(i, p - 1)

            def sum_squares(n, n_tok):
                for c in range(1, KC):
                    pool.wait_ge(h_sq_ready, n * KC + c + 1)
                    if c > 1:
                        pool.wait_ge(sq_add, n * (KC - 1) + c - 1)
                    pool.tensor_tensor(in_sq[:, 0:n_tok], mix[:, 0, 0:n_tok] if c == 1 else in_sq[:, 0:n_tok],
                                       mix[:, c, 0:n_tok], ALU.add).then_inc(sq_add, 1)

            for seg in segs:
                body(seg, 0)
                if seg.sublayer:
                    sum_squares(seg.sublayer, TOK if seg.sublayer < 5 else GRID)
                if seg.iters > 1:
                    with pool.Fori(1, seg.iters) as i:
                        body(seg, i)

        @block.scalar
        def _(act):
            act.dma_start(gains[:], gains_t).then_inc(gains_loaded, 16)
            for part, cs in enumerate((slice(0, X_FIRST), slice(X_FIRST, KC))):
                act.dma_start(h[:, cs, :], x_t[:, cs, :]).then_inc(x_loaded[part], 16)

            def split_hi(seg, i, p):
                n = seg.blocks * P
                act.wait_ge(loaded[p], seg.use(i, p) * 16)
                wait(act, unit_done, seg.former(i, p))
                act.activation(w_hi[:, p, 0:n], w_raw[:, p, 0:n], ACT.Copy).then_inc(w_hi_ready, 1)

            def ahead(seg, i, p):
                nxt, ni = (seg, i + 1) if not (isinstance(i, int) and i == seg.iters - 1) else (seg.next, 0)
                if nxt is None:
                    return
                for q in [p] if p < seg.body - 1 else range(p, nxt.body):
                    if q < nxt.body:
                        split_hi(nxt, ni, q)

            def prenorm(n, gain, n_tok):
                for c in range(KC):
                    if n == 0:
                        act.wait_ge(x_loaded[int(c >= X_FIRST)], 16)
                    else:
                        act.wait_ge(h_ready, (n - 1) * KC + c + 1)
                    act.activation(x_hi[:, c, 0:n_tok], h[:, c, 0:n_tok], ACT.Copy,
                                   scale=gains[:, gain, c:c + 1]).then_inc(x_hi_ready, 1)
                    act.activation(mix[:, c, 0:n_tok], h[:, c, 0:n_tok], ACT.Square).then_inc(h_sq_ready, 1)
                    if n == 0 and c in (1, 3):
                        split_hi(segs[0], 0, 2 + c // 2)

            def pre_std(n, n_tok):
                act.wait_ge(pre_mean_done, n + 1)
                tiles = len(token_tiles(n_tok))
                act.activation(std_rows[:, 0:tiles], bank[7][:, 0:tiles], ACT.Sqrt, bias=eps[:, 0:1]).then_inc(pre_std_ready, 1)

            def pre_rinv(n, n_tok):
                act.wait_ge(pre_spread, n + 1)
                act.activation(rinv[:, 0:n_tok], bank[7][:, SPREAD:SPREAD + n_tok], ACT.Copy).then_inc(rinv_ready, 1)

            def out_square(n, m, par, b, units, n_tok):
                act.wait_ge(unit_done, units)
                wait(act, out_sum_ready, m + (n * KC - 1))
                act.activation(out_sq[:, par, 0:n_tok], bank[b][:, 0:n_tok], ACT.Square).then_inc(out_sq_ready, 1)

            def post_std(n, n_tok):
                act.wait_ge(post_mean_done, n + 1)
                tiles = len(token_tiles(n_tok))
                act.activation(std_rows[:, 0:tiles], bank[7][:, 0:tiles], ACT.Sqrt, bias=eps[:, 0:1]).then_inc(post_std_ready, 1)

            def out_tiles(n, seg, n_tok):
                units = 2 if seg.name == "down" else 1
                per = seg.body // units

                def emit(i):
                    for t in range(per):
                        ps = range(t * units, (t + 1) * units)
                        last = isinstance(i, int) and i == seg.iters - 1 and t == per - 1
                        if last:
                            for p in ps[:-1]:
                                ahead(seg, i, p)
                            act.activation(warm[:, :], eps[:, :], ACT.Sqrt)
                        out_square(n, i * per + t, t % 2, out_bank(seg, i, t), seg.unit(i, (t + 1) * units - 1) + 1, n_tok)
                        if last:
                            post_std(n, n_tok)
                        for p in ps[-1:] if last else ps:
                            ahead(seg, i, p)
                bodies(act, seg, emit)

            def ffn(n, f, gain, n_tok):
                prenorm(n, gain, n_tok)
                up, down = plan["ffn", f]

                def emit(i):
                    for t in range(2):
                        ahead(up, i, 2 * t)
                        if isinstance(i, int) and i == 0 and t == 0:
                            pre_std(n, n_tok)
                            ahead(up, i, 2 * t + 1)
                            pre_rinv(n, n_tok)
                        tile = i * 2 + (f * FT + t)
                        act.wait_ge(g_ready, tile + 1)
                        act.activation(s_sb[:, t, 0:n_tok], g_sb[:, t, 0:n_tok], ACT.Silu).then_inc(silu_ready, 1)
                        if not (isinstance(i, int) and i == 0 and t == 0):
                            ahead(up, i, 2 * t + 1)
                bodies(act, up, emit)
                out_tiles(n, down, n_tok)

            def probT_copy(e, b, meta_width):
                act.wait_ge(probT_done, e + 1)
                act.activation(probT[:, b, :, :], bank[5][:, 0:QT * GRID].rearrange("p (a k) -> p a k", a=QT),
                               ACT.Copy).then_inc(probT_ready, 1)
                act.activation(probT_m[:, b, 0:meta_width], bank[6][0:META, 0:meta_width], ACT.Copy).then_inc(probT_ready, 1)

            def na(n, gain, n_tok):
                prenorm(n, gain, n_tok)
                seg = plan["na"]

                def exps(e, b):
                    act.wait_ge(top_ready, e + 1)
                    for t in range(QT):
                        act.activation(prob[:, b, t, :], prob[:, b, t, :], ACT.Exp, bias=ntop[:, b, t:t + 1],
                                       accum_out=rows[:, b, t:t + 1]).then_inc(exp_ready, 1)

                def former_pair_out(c):
                    act.wait_ge(heads_done, c)
                    act.activation(y_hi[:, bass.ds(c - 1, 1), :], bank[7][:, 0:TOK], ACT.Copy).then_inc(o_hi_ready, 1)

                def emit(c):
                    zero = isinstance(c, int) and c == 0
                    if not zero:
                        probT_copy(c * 2 - 2, 0, TOK)
                    ahead(seg, c, 0)
                    if zero:
                        pre_std(n, n_tok)
                        ahead(seg, c, 1)
                        pre_rinv(n, n_tok)
                    if not zero:
                        probT_copy(c * 2 - 1, 1, TOK)
                    exps(c * 2, 0)
                    if not zero:
                        ahead(seg, c, 1)
                    ahead(seg, c, 2)
                    exps(c * 2 + 1, 1)
                    act.wait_ge(m_step, c * 5 + 2)
                    act.activation(m_prob[:, :, :], m_prob[:, :, :], ACT.Exp).then_inc(m_exp_ready, 1)
                    act.wait_ge(turned, c + 1)
                    act.activation(v_s[:, 0:2, 0, :], bank[2][:, 0:2 * P].rearrange("p (a k) -> p a k", a=2),
                                   ACT.Copy).then_inc(v_ready, 1)
                    act.activation(v_s[0:META, 2, 0, :], bank[2][0:META, 2 * P:3 * P], ACT.Copy).then_inc(v_ready, 1)
                    if not zero:
                        former_pair_out(c)
                bodies(act, seg, emit)
                probT_copy(HEADS - 2, 0, TOK)
                probT_copy(HEADS - 1, 1, TOK)
                former_pair_out(HEADS // 2)
                out_tiles(n, plan["na_o"], n_tok)

            def gqa(n, gain, n_tok):
                prenorm(n, gain, TOK)
                kv, qs = plan["gqa_kv"], plan["gqa_q"]

                def square(j, w):
                    act.wait_ge(raw_ready, j + 1)
                    wait(act, head_mean_done, j - 1)
                    act.activation(u_sb[:, j % 2, 0:w], g_sb[:, j % 2, 0:w], ACT.Square).then_inc(raw_sq_ready, 1)

                def head_rms(j, w):
                    act.wait_ge(head_mean_done, j + 1)
                    wait(act, head_inv_ready, j)
                    tiles = len(token_tiles(w))
                    act.activation(head_std[:, 0:tiles, :], bank[2][:, 0:2 * tiles].rearrange("p (t b) -> p t b", b=2),
                                   ACT.Sqrt, bias=eps[:, 0:1]).then_inc(head_std_ready, 1)

                ahead(kv, 0, 0)
                pre_std(n, TOK)
                ahead(kv, 0, 1)
                pre_rinv(n, TOK)
                square(0, TOK)
                square(1, TOK)
                ahead(kv, 0, 2)
                for j in range(KC + 2):
                    head_rms(j, TOK if j < 2 else GRID)
                    if j == 0:
                        for x in range(2):
                            act.wait_ge(turned, HEADS // 2 + x + 1)
                            act.activation(v_s[:, 0:2, x, :], bank[5 + x][:, 0:2 * P].rearrange("p (a k) -> p a k", a=2),
                                           ACT.Copy).then_inc(v_ready, 1)
                            act.activation(v_s[0:META, 2, x, :], bank[5 + x][0:META, 2 * P:3 * P], ACT.Copy).then_inc(v_ready, 1)
                        ahead(kv, 0, 3)
                    elif j <= KC:
                        ahead(qs, (j - 1) // 4, (j - 1) % 4)
                    if j < KC:
                        square(j + 2, GRID)

                def chunk_out(chunk, x):
                    act.wait_ge(heads_done, chunk + (HEADS // 2 + 1))
                    act.activation(y_hi[:, bass.ds(chunk, 1), 0:GRID], bank[GQA_OUT[x]][:, 0:GRID], ACT.Copy).then_inc(o_hi_ready, 1)

                def step(s, x, b, do_t, do_s, do_out):
                    e = s * 2 + (HEADS + b)
                    if do_t:
                        probT_copy(e - 2, b, GRID)
                    if do_out and b == 1:
                        chunk_out(s - 2, x)
                    if do_s:
                        act.wait_ge(top_ready, e + 1)
                        for t in range(QT):
                            act.activation(prob[:, b, t, :], bank[2 * b + t][:, 0:TOK], ACT.Exp, bias=ntop[:, b, t:t + 1],
                                           accum_out=rows[:, b, t:t + 1]).then_inc(exp_ready, 1)
                for s in range(2):
                    for b in range(2):
                        step(s, s, b, s > 0, True, False)
                with act.Fori(1, HEADS // 4) as j:
                    for x in range(2):
                        for b in range(2):
                            step(j * 2 + x, x, b, True, True, True)
                for b in range(2):
                    step(KC, 0, b, True, False, True)
                chunk_out(KC - 1, 1)
                out_tiles(n, plan["gqa_o"], n_tok)

            split_hi(segs[0], 0, 0)
            split_hi(segs[0], 0, 1)
            act.wait_ge(gains_ready, 3)
            for n, kind, pre, post, n_tok in sublayers:
                if kind == "ffn":
                    ffn(n, ffn_of[n], pre, n_tok)
                elif kind == "na":
                    na(n, pre, n_tok)
                else:
                    gqa(n, pre, n_tok)

        @block.vector
        def _(dve):
            dve.memset(idle[:, :], 0.0).then_inc(idle_ready, 1)
            dve.memset(eps[:, :], EPS).then_inc(gains_ready, 1)
            dve.wait_ge(gains_loaded, 16)
            for post in (1, 5):
                dve.tensor_scalar(gains[:, post:12:6, :], gains[:, post:12:6, :], 0.5, None, ALU.mult).then_inc(gains_ready, 1)
            dve.wait_ge(gains_ready, 3)

            def split_lo(seg, i, p):
                dve.wait_ge(w_hi_ready, seg.unit(i, p) + 1)
                wait(dve, w_lo_ready, seg.unit(i, p))
                width = seg.blocks * P
                dve.tensor_tensor(w_lo[:, p, 0:width], w_raw[:, p, 0:width], w_hi[:, p, 0:width].bitcast(F32),
                                  ALU.subtract).then_inc(w_lo_ready, 1)

            for p in range(2):
                split_lo(segs[0], 0, p)

            def x_low(n, gain, c, n_tok):
                dve.wait_ge(x_hi_ready, n * KC + c + 1)
                dve.scalar_tensor_tensor(x_lo[:, c, 0:n_tok], h[:, c, 0:n_tok], gains[:, gain, c:c + 1],
                                         x_hi[:, c, 0:n_tok].bitcast(F32), ALU.mult, ALU.subtract).then_inc(x_lo_ready, 1)

            def input_rinv(n, n_tok, seg=None):
                tiles = len(token_tiles(n_tok))
                dve.wait_ge(pre_std_ready, n + 1)
                dve.reciprocal(inv_rows[:, 0:tiles], std_rows[:, 0:tiles]).then_inc(pre_inv_ready, 1)
                if seg:
                    split_lo(seg, 1, 0)
                dve.wait_ge(rinv_ready, n + 1)

            def out_tiles(n, seg, gain, n_tok):
                per = seg.body // (2 if seg.name == "down" else 1)

                def emit(i):
                    for t in range(per):
                        m, par = i * per + t, t % 2
                        dve.wait_ge(unit_done, seg.unit(i, (t + 1) * (seg.body // per) - 1) + 1)
                        dve.wait_ge(out_sq_ready, m + (n * KC + 1))
                        if isinstance(m, int) and m == 0:
                            dve.tensor_copy(sq_sum[:, 0:n_tok], out_sq[:, par, 0:n_tok]).then_inc(out_sum_ready, 1)
                        else:
                            dve.wait_ge(out_sum_ready, m + n * KC)
                            dve.tensor_tensor(sq_sum[:, 0:n_tok], sq_sum[:, 0:n_tok], out_sq[:, par, 0:n_tok],
                                              ALU.add).then_inc(out_sum_ready, 1)
                        dve.tensor_scalar(mix[:, bass.ds(m, 1), 0:n_tok], bank[out_bank(seg, i, t)][:, 0:n_tok].rearrange("p (a k) -> p a k", a=1),
                                          gains[:, gain, bass.ds(m, 1)], None, ALU.mult).then_inc(mix_ready, 1)
                        if t == 0 and seg.name in VECTOR_SPLITS and not (isinstance(i, int) and i == seg.iters - 1):
                            split_lo(seg, i + 1, 0)
                bodies(dve, seg, emit)

            def update(n, next_gain, n_tok):
                tiles = len(token_tiles(n_tok))
                dve.wait_ge(post_std_ready, n + 1)
                dve.reciprocal(inv_rows[:, 0:tiles], std_rows[:, 0:tiles]).then_inc(post_inv_ready, 1)

                def delta(c):
                    dve.tensor_tensor(mix[:, c, 0:n_tok], mix[:, c, 0:n_tok], bank[7][:, SPREAD:SPREAD + n_tok],
                                      ALU.mult).then_inc(delta_ready, 1)
                dve.wait_ge(post_spread, n + 1)
                dve.wait_ge(mix_ready, (n + 1) * KC)
                delta(0)
                for c in range(KC):
                    if 0 < c < KC - 1:
                        delta(c + 1)
                    dve.wait_ge(delta_ready, n * KC + c + 1)
                    dve.tensor_tensor(h[:, c, 0:n_tok], h[:, c, 0:n_tok], mix[:, c, 0:n_tok], ALU.add).then_inc(h_ready, 1)
                    if c == 0:
                        delta(1)
                    if c and next_gain is not None:
                        x_low(n + 1, next_gain, c - 1, n_tok)
                if next_gain is not None:
                    x_low(n + 1, next_gain, KC - 1, n_tok)

            def ffn(n, f, post, n_tok):
                up, down = plan["ffn", f]
                input_rinv(n, n_tok, up)

                def emit(i):
                    zero = isinstance(i, int) and i == 0
                    banks = FIRST_BANKS if zero else range(4)
                    for t in range(2):
                        j = i * 2 + t
                        tile = i * 2 + (f * FT + t)
                        dve.wait_ge(unit_done, up.unit(i, 2 * t) + 1)
                        dve.tensor_tensor(g_sb[:, t, 0:n_tok], bank[banks[2 * t]][:, 0:n_tok], rinv[:, 0:n_tok], ALU.mult).then_inc(g_ready, 1)
                        dve.wait_ge(unit_done, up.unit(i, 2 * t + 1) + 1)
                        dve.tensor_tensor(u_sb[:, t, 0:n_tok], bank[banks[2 * t + 1]][:, 0:n_tok], rinv[:, 0:n_tok], ALU.mult).then_inc(u_ready, 1)
                        if t == 0 and not zero and not (isinstance(i, int) and i == up.iters - 1):
                            split_lo(up, i + 1, 0)
                        dve.wait_ge(u_ready, tile + 1)
                        dve.wait_ge(silu_ready, tile + 1)
                        dve.tensor_tensor(f_sb[:, t, 0:n_tok], s_sb[:, t, 0:n_tok], u_sb[:, t, 0:n_tok], ALU.mult).then_inc(f_ready, 1)
                        dve.wait_ge(f_ready, tile + 1)
                        dve.tensor_copy(y_hi[:, bass.ds(j, 1), 0:n_tok], f_sb[:, t:t + 1, 0:n_tok]).then_inc(y_hi_ready, 1)
                        dve.wait_ge(y_hi_ready, tile + 1)
                        dve.tensor_tensor(y_lo[:, bass.ds(j, 1), 0:n_tok], f_sb[:, t:t + 1, 0:n_tok],
                                          y_hi[:, bass.ds(j, 1), 0:n_tok].bitcast(F32), ALU.subtract).then_inc(y_ready, 1)
                bodies(dve, up, emit)
                out_tiles(n, down, post, n_tok)

            def normalise(e, b):
                dve.wait_ge(exp_ready, e * 2 + 2)
                dve.reciprocal(rinv_rows[:, b, :], rows[:, b, :]).then_inc(sum_inv_ready, 1)
                dve.wait_ge(sum_inv_ready, e + 1)
                for t in range(QT):
                    dve.tensor_scalar(prob[:, b, t, :], prob[:, b, t, :], rinv_rows[:, b, t:t + 1], None,
                                      ALU.mult).then_inc(prob_ready, 1)

            def out_low(chunk, ps, o_chunk, n_tok):
                dve.wait_ge(o_hi_ready, chunk)
                dve.tensor_tensor(y_lo[:, bass.ds(o_chunk, 1), 0:n_tok], ps[:, 0:n_tok].rearrange("p (a k) -> p a k", a=1),
                                  y_hi[:, bass.ds(o_chunk, 1), 0:n_tok].bitcast(F32), ALU.subtract).then_inc(o_ready, 1)

            def na(n, post, n_tok):
                input_rinv(n, n_tok)
                seg = plan["na"]

                def value_product(c):
                    dve.wait_ge(unit_done, seg.unit(c, 2) + 1)
                    dve.tensor_tensor(vt_s[:, 0, :], bank[2][:, 0:TOK], rinv[:, :], ALU.mult).then_inc(vt_ready, 1)

                def emit(c):
                    zero = isinstance(c, int) and c == 0
                    dve.wait_ge(unit_done, seg.unit(c, 0) + 1)
                    dve.scalar_tensor_tensor(q_s[:, 0, :], bank[0][:, 0:TOK], SCALE, rinv[:, :], ALU.mult, ALU.mult).then_inc(q_ready, 1)
                    dve.wait_ge(unit_done, seg.unit(c, 1) + 1)
                    dve.tensor_tensor(k_s[:, 0, :], bank[1][:, 0:TOK], rinv[:, :], ALU.mult).then_inc(k_ready, 1)
                    if zero:
                        value_product(c)
                    for b in range(2):
                        e = c * 2 + b
                        if b == 1:
                            if not zero:
                                value_product(c)
                            normalise(c * 2, 0)
                        dve.wait_ge(bias_ready, e + 1)
                        dve.wait_ge(scores_done, e + 1)
                        for t in range(QT):
                            biased = dve.tensor_tensor(prob[:, b, t, :], bank[3 + t][:, 0:TOK], bias[:, b, t, :], ALU.add)
                        biased.then_inc(biased_ready, 1)
                        dve.wait_ge(biased_ready, e + 1)
                        dve.tensor_reduce(ntop[:, b, :], prob[:, b, :, :], AX.X, ALU.max, negate=True).then_inc(top_ready, 1)
                    dve.wait_ge(m_scores_done, c + 1)
                    meta = bank[6][0:META, META_AT:META_AT + 2 * META].rearrange("p (b k) -> p b k", b=2)
                    dve.tensor_reduce(m_top[:, :], meta, AX.X, ALU.max).then_inc(m_step, 1)
                    dve.wait_ge(m_step, c * 5 + 1)
                    wait(dve, probT_done, c * 2)
                    dve.tensor_tensor(m_prob[:, :, :], meta, m_top[:, :].unsqueeze(2).to_broadcast([META, 2, META]),
                                      ALU.subtract).then_inc(m_step, 1)
                    dve.wait_ge(m_exp_ready, c + 1)
                    dve.tensor_reduce(m_rows[:, :], m_prob[:, :, :], AX.X, ALU.add).then_inc(m_step, 1)
                    dve.wait_ge(m_step, c * 5 + 3)
                    dve.reciprocal(m_rinv[:, :], m_rows[:, :]).then_inc(m_step, 1)
                    dve.wait_ge(m_step, c * 5 + 4)
                    dve.tensor_tensor(m_prob[:, :, :], m_prob[:, :, :], m_rinv[:, :].unsqueeze(2).to_broadcast([META, 2, META]),
                                      ALU.mult).then_inc(m_step, 1)
                    if not zero:
                        out_low(c, bank[7], c - 1, TOK)
                    normalise(c * 2 + 1, 1)
                bodies(dve, seg, emit)
                out_low(HEADS // 2, bank[7], HEADS // 2 - 1, TOK)
                out_tiles(n, plan["na_o"], post, n_tok)

            def gqa(n, post, n_tok):
                input_rinv(n, TOK)
                kv, qs = plan["gqa_kv"], plan["gqa_q"]

                def evacuate(j, unit, ps, w):
                    dve.wait_ge(unit_done, unit + 1)
                    dve.tensor_tensor(g_sb[:, j % 2, 0:w], ps[:, 0:w], rinv[:, 0:w], ALU.mult).then_inc(raw_ready, 1)

                def head_rinv(j, w):
                    tiles = len(token_tiles(w))
                    dve.wait_ge(head_std_ready, j + 1)
                    wait(dve, head_spread, j)
                    dve.reciprocal(head_inv[:, 0:tiles, :], head_std[:, 0:tiles, :]).then_inc(head_inv_ready, 1)

                def norm(j, w):
                    dve.wait_ge(head_spread, j + 1)
                    dve.scalar_tensor_tensor(s_sb[:, j % 2, 0:w], g_sb[:, j % 2, 0:w], hgain[:, 1:2] if j < 2 else hgain[:, 0:1],
                                             bank[7][:, SPREAD:SPREAD + w], ALU.mult, ALU.mult).then_inc(normed_ready, 1)
                    dve.wait_ge(normed_ready, j + 1)
                    dve.tensor_tensor(f_sb[:, j % 2, 0:w], s_sb[:, j % 2, 0:w], cos_t[:, 0:w], ALU.mult).then_inc(cos_ready, 1)

                def rope(j, w):
                    dve.wait_ge(turn_done, j + 1)
                    dve.tensor_tensor(sine[:, 0:w], bank[4][:, 0:w], sin_t[:, 0:w], ALU.mult).then_inc(sin_ready, 1)
                    dve.wait_ge(sin_ready, j + 1)
                    dve.wait_ge(cos_ready, j + 1)
                    dst = k_s[:, j, 0:w] if j < 2 else q_all[:, j - 2, 0:w]
                    dve.tensor_tensor(dst, f_sb[:, j % 2, 0:w], sine[:, 0:w], ALU.add).then_inc(rope_ready, 1)

                def current(s, x):
                    wait(dve, scores_done, (s - 1) * 2 + HEADS)
                    dve.tensor_copy(q_s[:, x:x + 1, 0:GRID], q_all[:, bass.ds(s, 1), :]).then_inc(q_cur_ready, 1)

                def maxima(e, b):
                    dve.wait_ge(scores_done, e + 1)
                    for t in range(QT):
                        red = dve.tensor_reduce(ntop[:, b, t:t + 1], bank[2 * b + t][:, 0:TOK], AX.X, ALU.max, negate=True)
                    red.then_inc(top_ready, 1)

                evacuate(0, kv.unit(0, 0), bank[0], TOK)
                evacuate(1, kv.unit(0, 1), bank[1], TOK)
                for x in range(2):
                    dve.wait_ge(unit_done, kv.unit(0, 2 + x) + 1)
                    dve.tensor_tensor(vt_s[:, x, :], bank[5 + x][:, 0:TOK], rinv[:, :], ALU.mult).then_inc(vt_ready, 1)
                for j in range(KC + 2):
                    w = TOK if j < 2 else GRID
                    head_rinv(j, w)
                    if j:
                        rope(j - 1, TOK if j < 3 else GRID)
                    if j == KC + 1:
                        maxima(HEADS, 0)
                        dve.wait_ge(rope_ready, 4)
                        current(1, 1)
                    norm(j, w)
                    if j < KC:
                        evacuate(j + 2, qs.unit(0, 0) + j, bank[Q_BANKS[j % 3]], GRID)
                    if j == KC - 1:
                        dve.wait_ge(rope_ready, 3)
                        current(0, 0)
                normalise(HEADS, 0)
                maxima(HEADS + 1, 1)
                rope(KC + 1, GRID)
                dve.wait_ge(rope_ready, KC + 2)

                def chunk(s, x, out=True, last=False):
                    for b in range(2):
                        e = s * 2 + (HEADS + b)
                        normalise(e - 1, 1 - b)
                        maxima(e, b)
                        if b == 0 and not last:
                            current(s + 1, 1 - x)
                        if b == 1 and out:
                            out_low(s + (HEADS // 2 - 1), bank[GQA_OUT[x]], s - 2, GRID)

                chunk(1, 1, out=False)
                with dve.Fori(1, HEADS // 4 - 1) as j:
                    for x in range(2):
                        chunk(j * 2 + x, x)
                chunk(KC - 2, 0)
                chunk(KC - 1, 1, last=True)
                normalise(2 * HEADS - 1, 1)
                out_low(HEADS - 1, bank[GQA_OUT[0]], KC - 2, GRID)
                out_low(HEADS, bank[GQA_OUT[1]], KC - 1, GRID)
                out_tiles(n, plan["gqa_o"], post, n_tok)

            for c in range(KC):
                dve.wait_ge(x_loaded[int(c >= X_FIRST)], 16)
                x_low(0, 0, c, TOK)
                if c:
                    dve.wait_ge(h_sq_ready, c + 1)
                    if c > 1:
                        dve.wait_ge(sq_add, c - 1)
                    dve.tensor_tensor(in_sq[:, :], mix[:, 0, :] if c == 1 else in_sq[:, :], mix[:, c, :], ALU.add).then_inc(sq_add, 1)
            dve.wait_ge(const_loaded, 16)
            dve.tensor_scalar(hgain[:, 0:1], hgain[:, 0:1], SCALE, None, ALU.mult).then_inc(const_ready, 1)
            for n, kind, pre, post, n_tok in sublayers:
                if kind == "ffn":
                    ffn(n, ffn_of[n], post, n_tok)
                elif kind == "na":
                    na(n, post, n_tok)
                else:
                    gqa(n, post, n_tok)
                update(n, sublayers[n + 1][2] if n + 1 < len(sublayers) else None, n_tok)

        @block.tensor
        def _(pe):
            def product(ps, seg, p, k, rhs, n_tok, start, stop):
                (hi, lo), r = rhs
                w = slice(k * P, (k + 1) * P)
                pe.matmul(ps[:, 0:n_tok], w_hi[:, p, w], hi[:, r, 0:n_tok], start=start, stop=False)
                pe.matmul(ps[:, 0:n_tok], w_hi[:, p, w], lo[:, r, 0:n_tok], start=False, stop=False)
                return pe.matmul(ps[:, 0:n_tok], w_lo[:, p, w], hi[:, r, 0:n_tok], start=False, stop=stop)

            def unit(seg, i, p, ps, n_tok, act_in, r0=0, start=True, stop=True):
                pe.wait_ge(w_lo_ready, seg.unit(i, p) + 1)
                for k in range(seg.blocks):
                    mm = product(ps, seg, p, k, (act_in, r0 + k), n_tok, start and k == 0, stop and k == seg.blocks - 1)
                mm.then_inc(unit_done, 1)

            X, Y = (x_hi, x_lo), (y_hi, y_lo)

            def keep_clock(products):
                for _ in range(products):
                    pe.matmul(bank[2][:, 0:P], idle[:, :], idle[:, :], start=True, stop=True)

            def token_means(src, n_tok):
                for t, (t0, _) in enumerate(token_tiles(n_tok)):
                    mm = pe.matmul(bank[7][:, t:t + 1], src[:, t0:t0 + P], mean_w[:, :], start=True, stop=True)
                return mm

            def spread(n_tok):
                for t, (t0, first) in enumerate(token_tiles(n_tok)):
                    mm = pe.matmul(bank[7][:, SPREAD + first:SPREAD + t0 + P], inv_rows[:, t:t + 1].to_broadcast([P, P]),
                                   ident[:, first - t0:P], start=True, stop=True)
                return mm

            def first_units(n, seg, banks, n_tok):
                others = range(2, seg.body)
                pe.wait_ge(w_lo_ready, seg.unit(0, 1) + 1)
                waited = False
                for what in FIRST_ORDER if n else START_ORDER:
                    if what == "mean":
                        pe.wait_ge(sq_add, (n + 1) * (KC - 1))
                        pe.wait_ge(const_ready, 1)
                        token_means(in_sq, n_tok).then_inc(pre_mean_done, 1)
                        continue
                    if what == "spread":
                        pe.wait_ge(pre_inv_ready, n + 1)
                        spread(n_tok).then_inc(pre_spread, 1)
                        continue
                    part, k = what
                    if part == "a" and k == 0:
                        pe.wait_ge(x_hi_ready, n * KC + 1)
                        for w in (w_hi, w_lo):
                            for p in range(2):
                                pe.matmul(banks[p][:, 0:n_tok], w[:, p, 0:P], x_hi[:, 0, 0:n_tok], start=w is w_hi, stop=False)
                        pe.wait_ge(x_lo_ready, n * KC + 1)
                        for p in range(2):
                            pe.matmul(banks[p][:, 0:n_tok], w_hi[:, p, 0:P], x_lo[:, 0, 0:n_tok], start=False, stop=False)
                        continue
                    if part == "a":
                        pe.wait_ge(x_lo_ready, n * KC + k + 1)
                    elif not waited:
                        pe.wait_ge(w_lo_ready, seg.unit(0, seg.body - 1) + 1)
                        waited = True
                    for p in range(2) if part == "a" else others:
                        mm = product(banks[p], seg, p, k, (X, k), n_tok, k == 0, k == KC - 1)
                        if k == KC - 1:
                            mm.then_inc(unit_done, 1)

            def o_blocks(seg, t, k0, k1, n_tok):
                if k0 == 0:
                    pe.wait_ge(w_lo_ready, seg.unit(0, t) + 1)
                for k in range(k0, k1):
                    mm = product(bank[O_BANKS[t]], seg, t, k, (Y, k), n_tok, k == 0, k == KC - 1)
                if k1 == KC:
                    mm.then_inc(unit_done, 1)

            def out_tiles(n, seg, n_tok, ready, before):
                units = 2 if seg.name == "down" else 1
                per = seg.body // units

                def emit(i):
                    zero = isinstance(i, int) and i == 0
                    if zero and units == 1:
                        pe.wait_ge(ready, before + KC)
                        for t in range(3):
                            o_blocks(seg, t, KC - 1, KC, n_tok)
                    for t in range(3 if zero and units == 1 else 0, per):
                        m = i * per + t
                        if not (zero and units == 1):
                            wait(pe, mix_ready, m + (n * KC - 1))
                            wait(pe, out_sq_ready, m + (n * KC - 1))
                        for k in range(units):
                            if zero and t == 0:
                                pe.wait_ge(ready, before + (k + 1) * seg.blocks)
                            unit(seg, i, t * units + k, bank[out_bank(seg, i, t)], n_tok, Y, k * seg.blocks, k == 0, k == units - 1)
                bodies(pe, seg, emit)
                keep_clock(5)
                pe.wait_ge(out_sum_ready, (n + 1) * KC)
                token_means(sq_sum, n_tok).then_inc(post_mean_done, 1)
                pe.wait_ge(post_inv_ready, n + 1)
                spread(n_tok).then_inc(post_spread, 1)
                if n < len(sublayers) - 1:
                    keep_clock(8)

            def ffn(n, f, n_tok):
                up, down = plan["ffn", f]

                def emit(i):
                    if isinstance(i, int) and i == 0:
                        first_units(n, up, [bank[b] for b in FIRST_BANKS], n_tok)
                        return
                    for t in range(2):
                        tile = i * 2 + (f * FT + t)
                        pe.wait_ge(g_ready, tile - 1)
                        pe.wait_ge(u_ready, tile - 1)
                        unit(up, i, 2 * t, bank[2 * t], n_tok, X)
                        unit(up, i, 2 * t + 1, bank[2 * t + 1], n_tok, X)
                bodies(pe, up, emit)
                out_tiles(n, down, n_tok, y_ready, f * FT)

            def scores(e, b, x, ps):
                at = slice(HD * b, HD * (b + 1))
                for t in range(QT):
                    mm = pe.matmul(ps[t][:, 0:TOK], q_s[at, x[0], t * P:(t + 1) * P], k_s[at, x[1], :], start=True, stop=True)
                mm.then_inc(scores_done, 1)

            def transposed(e, b, meta_pair=None):
                wait(pe, probT_ready, e * 2)
                for t in range(QT):
                    pe.wait_ge(prob_ready, e * 2 + (t + 1))
                    for kc in range(2):
                        pe.transpose(bank[5][:, kc * GRID + t * P:kc * GRID + (t + 1) * P],
                                     prob[:, b, t, kc * P:(kc + 1) * P], ident[:, :])
                if meta_pair is not None:
                    pe.wait_ge(m_step, meta_pair * 5 + 5)
                for t in range(QT):
                    mm = pe.transpose(bank[6][0:META, t * P:(t + 1) * P], prob[:, b, t, GRID:TOK], ident[:, :])
                if meta_pair is not None:
                    mm = pe.transpose(bank[6][0:META, GRID:TOK], m_prob[:, b, :], ident[0:META, 0:META])
                mm.then_inc(probT_done, 1)

            def values(e, b, x, ps, width):
                pe.wait_ge(probT_ready, e * 2 + 2)
                at = slice(HD * b, HD * (b + 1))
                pe.matmul(ps[at, 0:width], v_s[0:META, 2, x, at], probT_m[:, b, 0:width], start=True, stop=False)
                for kc in range(2):
                    mm = pe.matmul(ps[at, 0:GRID], v_s[:, kc, x, at], probT[:, b, kc, :], start=False, stop=kc == 1)
                if b == 1:
                    mm.then_inc(heads_done, 1)

            def turn_values(x, vx, ps):
                for kc, (k0, k1) in enumerate(((0, P), (P, 2 * P), (GRID, TOK))):
                    mm = pe.transpose(ps[0:k1 - k0, kc * P:(kc + 1) * P], vt_s[:, x, k0:k1], ident[:, :])
                mm.then_inc(turned, 1)

            def na(n, n_tok):
                seg = plan["na"]

                def head(e, c, b):
                    transposed(e, b, c)

                def meta_scores(b):
                    at = slice(HD * b, HD * (b + 1))
                    return pe.matmul(bank[6][0:META, META_AT + META * b:META_AT + META * (b + 1)], q_s[at, 0, GRID:TOK],
                                     k_s[at, 0, GRID:TOK], start=True, stop=True)

                def blocks_of(c, p, ps, k0, k1):
                    for k in range(k0, k1):
                        mm = product(ps, seg, p, k, (X, k), TOK, k == 0, k == KC - 1)
                    if k1 == KC:
                        mm.then_inc(unit_done, 1)

                def emit(c):
                    zero = isinstance(c, int) and c == 0
                    if zero:
                        first_units(n, seg, bank[0:3], n_tok)
                    else:
                        pe.wait_ge(q_ready, c)
                        unit(seg, c, 0, bank[0], TOK, X)
                        pe.wait_ge(k_ready, c)
                        pe.wait_ge(w_lo_ready, seg.unit(c, 1) + 1)
                        blocks_of(c, 1, bank[1], 0, KC // 2)
                        head(c * 2 - 2, c - 1, 0)
                        blocks_of(c, 1, bank[1], KC // 2, KC)
                        wait(pe, o_ready, c - 1)
                        pe.wait_ge(v_ready, c * 2)
                        values(c * 2 - 2, 0, 0, bank[7], TOK)
                    pe.wait_ge(q_ready, c + 1)
                    pe.wait_ge(k_ready, c + 1)
                    wait(pe, biased_ready, c * 2)
                    if zero:
                        meta_scores(0)
                    scores(c * 2, 0, (0, 0), bank[3:5])
                    if not zero:
                        meta_scores(0)
                        head(c * 2 - 1, c - 1, 1)
                        unit(seg, c, 2, bank[2], TOK, X)
                        values(c * 2 - 1, 1, 0, bank[7], TOK)
                    pe.wait_ge(biased_ready, c * 2 + 1)
                    scores(c * 2 + 1, 1, (0, 0), bank[3:5])
                    meta_scores(1).then_inc(m_scores_done, 1)
                    pe.wait_ge(vt_ready, c + 1)
                    turn_values(0, 0, bank[2])
                bodies(pe, seg, emit)
                c, o = HEADS // 2, plan["na_o"]
                pe.wait_ge(o_ready, KC - 2)
                o_blocks(o, 0, 0, KC - 2, n_tok)
                head(c * 2 - 2, c - 1, 0)
                o_blocks(o, 1, 0, KC - 2, n_tok)
                pe.wait_ge(o_ready, KC - 1)
                pe.wait_ge(v_ready, c * 2)
                values(c * 2 - 2, 0, 0, bank[7], TOK)
                head(c * 2 - 1, c - 1, 1)
                for t in range(2):
                    o_blocks(o, t, KC - 2, KC - 1, n_tok)
                values(c * 2 - 1, 1, 0, bank[7], TOK)
                o_blocks(o, 2, 0, KC - 1, n_tok)
                out_tiles(n, plan["na_o"], n_tok, o_ready, 0)

            def gqa(n, n_tok):
                kv, qs = plan["gqa_kv"], plan["gqa_q"]

                def head_mean(j):
                    w = TOK if j < 2 else GRID
                    pe.wait_ge(raw_sq_ready, j + 1)
                    wait(pe, head_std_ready, j)
                    for t, (t0, _) in enumerate(token_tiles(w)):
                        mm = pe.matmul(bank[2][:, 2 * t:2 * t + 2], u_sb[:, j % 2, t0:t0 + P], head_mean_w[:, :], start=True, stop=True)
                    mm.then_inc(head_mean_done, 1)

                def spread_heads(j):
                    pe.wait_ge(head_inv_ready, j + 1)
                    wait(pe, normed_ready, j)
                    for t, (t0, first) in enumerate(token_tiles(TOK if j < 2 else GRID)):
                        for b in range(2):
                            mm = pe.matmul(bank[7][HD * b:HD * (b + 1), SPREAD + first:SPREAD + t0 + P],
                                           head_inv[:, t, b:b + 1].to_broadcast([P, HD]),
                                           ident[:, first - t0:P], start=True, stop=True)
                    mm.then_inc(head_spread, 1)

                def turn(j):
                    w = TOK if j < 2 else GRID
                    pe.wait_ge(normed_ready, j + 1)
                    wait(pe, sin_ready, j)
                    pe.matmul(bank[4][:, 0:w], turn_w[:, :], s_sb[:, j % 2, 0:w], start=True, stop=True).then_inc(turn_done, 1)

                def q_blocks(s, k0, k1):
                    for k in range(k0, k1):
                        mm = product(bank[Q_BANKS[s % 3]], qs, s % 4, k, (X, k), GRID, k == 0, k == KC - 1)
                    if k1 == KC:
                        mm.then_inc(unit_done, 1)

                def first_scores(b):
                    pe.wait_ge(q_cur_ready, 1)
                    pe.wait_ge(raw_ready, KC + 2)
                    scores(HEADS + b, b, (0, 0), bank[2 * b:2 * b + 2])

                first_units(n, kv, [bank[b] for b in (0, 1, 5, 6)], TOK)
                for j in range(KC + 2):
                    if j < KC:
                        wait(pe, raw_ready, j)
                        pe.wait_ge(w_lo_ready, qs.unit(0, 0) + j + 1)
                        q_blocks(j, 0, KC // 2)
                    head_mean(j)
                    if j:
                        turn(j - 1)
                    if j == KC:
                        first_scores(0)
                    if j < KC:
                        q_blocks(j, KC // 2, KC)
                    if j == 0:
                        pe.wait_ge(vt_ready, KC + 2)
                        for x in range(2):
                            turn_values(x, x, bank[5 + x])
                    spread_heads(j)
                first_scores(1)
                turn(KC + 1)
                pe.wait_ge(v_ready, HEADS + 4)

                def step(s, x, b, do_s=True, do_v=True):
                    e = s * 2 + (HEADS + b)
                    transposed(e - 2, b)
                    if do_s:
                        if b == 0:
                            pe.wait_ge(q_cur_ready, s + 1)
                        pe.wait_ge(exp_ready, e * 2 - 2)
                        scores(e, b, (x, x), bank[2 * b:2 * b + 2])
                    if do_v:
                        if b == 1:
                            wait(pe, o_ready, s + (HEADS // 2 - 2))
                        out_x = 1 - x if b == 1 else x
                        values(e - 3, 1 - b, out_x, bank[GQA_OUT[out_x]], GRID)

                for b in range(2):
                    step(1, 1, b, do_v=b > 0)
                with pe.Fori(1, HEADS // 4) as j:
                    for x in range(2):
                        for b in range(2):
                            step(j * 2 + x, x, b)
                o = plan["gqa_o"]
                for b in range(2):
                    step(KC, 0, b, do_s=False)
                    pe.wait_ge(o_ready, HEADS - 2)
                    o_blocks(o, b, 0, KC - 2, n_tok)
                values(2 * HEADS - 1, 1, 1, bank[GQA_OUT[1]], GRID)
                pe.wait_ge(o_ready, HEADS - 1)
                for t in range(2):
                    o_blocks(o, t, KC - 2, KC - 1, n_tok)
                o_blocks(o, 2, 0, KC - 1, n_tok)
                out_tiles(n, plan["gqa_o"], n_tok, o_ready, KC)

            pe.wait_ge(idle_ready, 1)
            keep_clock(22)
            for n, kind, pre, post, n_tok in sublayers:
                if kind == "ffn":
                    ffn(n, ffn_of[n], n_tok)
                elif kind == "na":
                    na(n, n_tok)
                else:
                    gqa(n, n_tok)


def blocks(w, tile_of=None):
    import numpy as np
    k, n = w.shape
    return np.ascontiguousarray(w.reshape(k // P, P, n // P, P).transpose(2, 1, 0, 3)).reshape(n // P, P, k)


def lay_out(a):
    import numpy as np
    f32 = np.float32
    tokens = np.concatenate([a["x"][0], a["meta_tokens"]])
    d = {"x_t": tokens.T.reshape(KC, P, TOK).transpose(1, 0, 2),
         "gains_t": a["norm_gains"].reshape(12, KC, P).transpose(2, 0, 1)}
    gate, up, down = (a[k].reshape(4, *a[k].shape[2:]) for k in ("ffn_w_gate", "ffn_w_up", "ffn_w_down"))
    d["ffn_up_w"] = np.stack([np.stack([blocks(gate[f]), blocks(up[f])], 1).reshape(2 * FT, P, D) for f in range(4)])
    d["ffn_down_w"] = np.stack([blocks(down[f]).reshape(KC, P, 2, WIDE * P).transpose(0, 2, 1, 3)
                                .reshape(2 * KC, P, WIDE * P) for f in range(4)])
    d["na_w"] = blocks(a["na_w_qkv"][0]).reshape(3, KC, P, D).transpose(1, 0, 2, 3).reshape(3 * KC, P, D)
    d["na_o_w"] = blocks(a["na_w_o"][0])
    order = [8 * x + 4 * b + j for j in range(4) for x in range(2) for b in range(2)]
    w = a["gqa_w_qkv"][0]
    wq = w[:, :D].reshape(D, HEADS, HD)[:, order].reshape(D, D)
    d["gqa_kv_w"] = blocks(w[:, D:])
    d["gqa_q_w"] = blocks(wq)
    d["gqa_o_w"] = blocks(a["gqa_w_o"][0].reshape(HEADS, HD, D)[order].reshape(D, D))
    d["rpb"], d["meta_bias"] = a["na_rpb"][0], a["na_meta_bias"][0]
    col = np.arange(GRID_W)
    start = np.clip(col - 8, 0, GRID_W - 16)[:, None]
    inside = (col[None] >= start) & (col[None] < start + 16)
    masked = np.tile(np.where(inside, 0.0, -2.0 ** 100).astype(f32), (2, GRID_H))
    window = np.concatenate([masked, np.zeros((P, META), f32)], 1)
    turn = np.zeros((P, P), f32)
    for m in range(P):
        if m % 32 < 16:
            turn[m + 16, m] = -1.0
        else:
            turn[m - 16, m] = 1.0
    sec = HD // 2
    freqs = f32(10000.0) ** (-np.arange(0, sec, 2, dtype=f32) / f32(sec))
    t = np.arange(GRID)
    ang = np.stack([(t // GRID_W).astype(f32)[:, None] * freqs, (t % GRID_W).astype(f32)[:, None] * freqs], 1)
    ang = np.concatenate([ang, np.zeros((META, 2, sec // 2), f32)])
    ang = np.tile(np.repeat(ang[:, :, None], 2, 2).reshape(TOK, HD), (1, 2)).T
    d["const_c"] = np.concatenate([
        np.eye(P, dtype=f32), np.full((P, 1), 1.0 / D, f32), np.kron(np.eye(2), np.full((HD, 1), 1.0 / HD)).astype(f32),
        turn, np.cos(ang, dtype=f32), np.sin(ang, dtype=f32), window,
        np.tile(a["gqa_q_gain"][0], 2)[:, None], np.tile(a["gqa_k_gain"][0], 2)[:, None]], 1)
    return {k: np.ascontiguousarray(v) for k, v in d.items()}


_ORDER = ["x_t", "gains_t", "ffn_up_w", "ffn_down_w", "na_w", "na_o_w", "gqa_kv_w", "gqa_q_w", "gqa_o_w",
          "rpb", "meta_bias", "const_c"]


def kernel(**inputs):
    import numpy as np
    import concourse.bacc as bacc
    from concourse.bass_utils import run_bass_kernel_spmd

    given = lay_out({k: np.asarray(v) for k, v in inputs.items()})
    nc = bacc.Bacc("TRN2", target_bir_lowering=False, num_devices=1)
    args = [nc.dram_tensor(k, given[k].shape, F32, kind="ExternalInput").ap() for k in _ORDER]
    args.append(nc.dram_tensor("out", (P, KC, GRID), F32, kind="ExternalOutput").ap())
    build(nc, *args)
    got = run_bass_kernel_spmd(nc, [given], core_ids=[0]).results[0]["out"]
    return got.transpose(2, 1, 0).reshape(1, GRID, D)
```
